# Optimizing a Trainium2 kernel written in Bass

```python
import jax, jax.numpy as jnp
from jax import lax
import numpy as np

D_MODEL = 2048
BATCH = 1
SEQ = 256
DEPTH = 1
DEC_BATCH = 8
DEC_SEQ = 4
PAST_LEN = 2048
PAGE_SIZE = 128

MIX_WIDTH = D_MODEL
A_WIDTH = MIX_WIDTH // 2
A_GROUPS = 8
A_GROUP_DIM = A_WIDTH // A_GROUPS
A_CHUNK = 128
B_HEADS = 8
B_KEY_DIM = (MIX_WIDTH - A_WIDTH) // B_HEADS
B_VAL_DIM = B_KEY_DIM
B_WIDTH = B_HEADS * B_VAL_DIM
CONV_W = 4
CONV_DIM = 2 * B_HEADS * B_KEY_DIM + B_WIDTH
DN_CHUNK = 64
IN_DIM = 2 * A_WIDTH + CONV_DIM + B_WIDTH + 2 * B_HEADS
N_GROUPS = 4
EXPERTS_PER_GROUP = 8
N_EXPERTS = N_GROUPS * EXPERTS_PER_GROUP
TOP_K = 2
D_EXPERT = D_MODEL // 4
MOE_BLOCK = 128
PLE_DIM = 256
EPS = 1e-6

kernel_name = "hymba_chunkmlp_gdn_hmoe_ple_step"

def rms_norm(x, g):
    xf = x.astype(jnp.float32)
    y = xf * lax.rsqrt(jnp.mean(xf * xf, axis=-1, keepdims=True) + EPS)
    return (y * g.astype(jnp.float32)).astype(x.dtype)

def group_layer_norm(v, g):
    vf = v.astype(jnp.float32)
    mu = jnp.mean(vf, axis=-1, keepdims=True)
    d = vf - mu
    var = jnp.mean(d * d, axis=-1, keepdims=True)
    return (d * lax.rsqrt(var + EPS) * g.astype(jnp.float32)).astype(v.dtype)

def l2_norm(x):
    xf = x.astype(jnp.float32)
    return xf * lax.rsqrt(jnp.sum(xf * xf, axis=-1, keepdims=True) + EPS)

def chunk_spatial_gate(u, v, w_s, b_s):
    Bn, L, H, Cd = v.shape
    causal = jnp.tril(jnp.ones((A_CHUNK, A_CHUNK), dtype=bool))
    w = jnp.where(causal, w_s, 0).astype(v.dtype)
    b = b_s.astype(v.dtype)
    if L < A_CHUNK:
        mixed = jnp.einsum('hts,bshc->bthc', w[:, :L, :L], v) + b[:, :L].T[:, :, None]
    else:
        n = -(-L // A_CHUNK)
        vp = jnp.pad(v, ((0, 0), (0, n * A_CHUNK - L), (0, 0), (0, 0))).reshape(Bn, n, A_CHUNK, H, Cd)
        mixed = (jnp.einsum('hts,bnshc->bnthc', w, vp) + b.T[:, :, None]).reshape(Bn, n * A_CHUNK, H, Cd)[:, :L]
    return u * mixed

def short_conv(xs, buf, w):
    L = xs.shape[1]
    xp = jnp.concatenate([buf.astype(xs.dtype), xs], axis=1)
    y = xp[:, 0:L] * w[0].astype(xs.dtype)
    for j in range(1, CONV_W):
        y = y + xp[:, j:j + L] * w[j].astype(xs.dtype)
    return jax.nn.silu(y), xp[:, L:]

def gated_delta_rule(q, k, v, g, beta, s0):
    f32 = jnp.float32
    Bn, L, H, DK = q.shape
    DV = v.shape[-1]
    C = DN_CHUNK if L >= DN_CHUNK else L
    n = -(-L // C)
    pad = n * C - L

    def prep(t):
        t = jnp.pad(t.astype(f32), [(0, 0), (0, pad)] + [(0, 0)] * (t.ndim - 2))
        t = t.reshape((Bn, n, C) + t.shape[2:])
        return jnp.moveaxis(t, 3, 1)

    q = prep(q) * (DK ** -0.5)
    k, v, g, beta = prep(k), prep(v), prep(g), prep(beta)
    G = jnp.cumsum(g, axis=-1)
    causal = jnp.tril(jnp.ones((C, C), dtype=bool))
    strict = jnp.tril(jnp.ones((C, C), dtype=bool), -1)
    decay = jnp.exp(jnp.where(causal, G[..., :, None] - G[..., None, :], -jnp.inf))
    kb = k * beta[..., None]
    a_mat = jnp.where(strict, jnp.einsum('bhnid,bhnjd->bhnij', kb, k) * decay, 0.0)
    m = a_mat + jnp.eye(C, dtype=f32)
    u = lax.linalg.triangular_solve(m, v * beta[..., None], left_side=True, lower=True, unit_diagonal=True)
    w = lax.linalg.triangular_solve(m, kb * jnp.exp(G)[..., None], left_side=True, lower=True, unit_diagonal=True)
    qk = jnp.einsum('bhnid,bhnjd->bhnij', q, k) * decay
    qg = q * jnp.exp(G)[..., None]
    kd = k * jnp.exp(G[..., -1:] - G)[..., None]
    gl = jnp.exp(G[..., -1])

    def step(S, inp):
        qg_c, kd_c, u_c, w_c, qk_c, gl_c = inp
        v_new = u_c - jnp.einsum('bhck,bhkv->bhcv', w_c, S)
        o = jnp.einsum('bhck,bhkv->bhcv', qg_c, S) + jnp.einsum('bhij,bhjv->bhiv', qk_c, v_new)
        S = S * gl_c[..., None, None] + jnp.einsum('bhck,bhcv->bhkv', kd_c, v_new)
        return S, o

    xs = tuple(jnp.moveaxis(t, 2, 0) for t in (qg, kd, u, w, qk, gl))
    S, o = lax.scan(step, s0.astype(f32), xs)
    o = jnp.transpose(o, (1, 0, 3, 2, 4)).reshape(Bn, n * C, H, DV)[:, :L]
    return o, S

def swiglu(xb, wg, wu, wd):
    return (jax.nn.silu(xb @ wg.astype(xb.dtype)) * (xb @ wu.astype(xb.dtype))) @ wd.astype(xb.dtype)

def hier_moe(h, w_group, b_group, w_router, b_router, w_gate, w_up, w_down):
    T, D = h.shape
    hf = h.astype(jnp.float32)
    g_logits = hf @ w_group.astype(jnp.float32) + b_group.astype(jnp.float32)
    g_prob = jax.nn.softmax(g_logits, axis=-1)
    g_sel = jnp.argmax(g_logits, axis=-1)
    g_w = jnp.take_along_axis(g_prob, g_sel[:, None], axis=1)
    e_logits = (hf @ w_router.astype(jnp.float32) + b_router.astype(jnp.float32)).reshape(T, N_GROUPS, EXPERTS_PER_GROUP)
    e_in_group = jnp.take_along_axis(e_logits, g_sel[:, None, None], axis=1)[:, 0]
    top_v, top_i = lax.top_k(e_in_group, TOP_K)
    weight = g_w * jax.nn.softmax(top_v, axis=-1)
    expert_id = g_sel[:, None] * EXPERTS_PER_GROUP + top_i

    n_assign = T * TOP_K
    flat_e = expert_id.reshape(-1).astype(jnp.int32)
    flat_w = weight.reshape(-1)
    flat_tok = jnp.repeat(jnp.arange(T, dtype=jnp.int32), TOP_K)
    order = jnp.argsort(flat_e)
    e_sorted = flat_e[order]
    counts = jnp.zeros((N_EXPERTS,), jnp.int32).at[flat_e].add(1)
    padded = (counts + MOE_BLOCK - 1) // MOE_BLOCK * MOE_BLOCK
    pad_end = jnp.cumsum(padded)
    pad_start = pad_end - padded
    start = jnp.cumsum(counts) - counts
    rank = jnp.arange(n_assign, dtype=jnp.int32) - start[e_sorted]
    dest = pad_start[e_sorted] + rank
    n_blocks = -(-n_assign // MOE_BLOCK) + N_EXPERTS
    n_rows = n_blocks * MOE_BLOCK
    row_tok = jnp.zeros((n_rows,), jnp.int32).at[dest].set(flat_tok[order])
    row_w = jnp.zeros((n_rows,), h.dtype).at[dest].set(flat_w[order].astype(h.dtype))
    block_e = jnp.minimum(jnp.searchsorted(pad_end, jnp.arange(n_blocks, dtype=jnp.int32) * MOE_BLOCK, side='right'),
                          N_EXPERTS - 1).astype(jnp.int32)
    xb = h[row_tok].reshape(n_blocks, MOE_BLOCK, D)

    def block_ffn(args):
        x_blk, e = args
        return swiglu(x_blk, w_gate[e], w_up[e], w_down[e])

    yb = lax.map(block_ffn, (xb, block_e)).reshape(n_rows, D)
    return jax.ops.segment_sum(yb * row_w[:, None], row_tok, num_segments=T)

def hybrid_layer(x, p, conv_buf, s0, g_mix, w_in, w_s, b_s, g_v, conv_w, a_log, dt_bias, g_out, w_out,
                 g_ffn, w_group, b_group, w_router, b_router, w_gate, w_up, w_down, g_ple, w_ple_gate, w_ple):
    Bn, L, D = x.shape
    h = rms_norm(x, g_mix)
    proj = h @ w_in.astype(x.dtype)
    s1 = A_WIDTH
    s2 = 2 * A_WIDTH
    s3 = s2 + CONV_DIM
    s4 = s3 + B_WIDTH
    s5 = s4 + B_HEADS
    a_u, a_v, qkv, z, a_dec, b_beta = jnp.split(proj, [s1, s2, s3, s4, s5], axis=-1)

    u = jax.nn.gelu(a_u).reshape(Bn, L, A_GROUPS, A_GROUP_DIM)
    v_a = group_layer_norm(jax.nn.gelu(a_v).reshape(Bn, L, A_GROUPS, A_GROUP_DIM), g_v)
    out_a = chunk_spatial_gate(u, v_a, w_s, b_s).reshape(Bn, L, A_WIDTH)

    qkv, new_buf = short_conv(qkv, conv_buf, conv_w)
    q, k, v = jnp.split(qkv, [B_HEADS * B_KEY_DIM, 2 * B_HEADS * B_KEY_DIM], axis=-1)
    q = l2_norm(q.reshape(Bn, L, B_HEADS, B_KEY_DIM))
    k = l2_norm(k.reshape(Bn, L, B_HEADS, B_KEY_DIM))
    v = v.reshape(Bn, L, B_HEADS, B_VAL_DIM)
    beta = jax.nn.sigmoid(b_beta.astype(jnp.float32))
    g = -jnp.exp(a_log.astype(jnp.float32)) * jax.nn.softplus(a_dec.astype(jnp.float32) + dt_bias.astype(jnp.float32))
    o, s_new = gated_delta_rule(q, k, v, g, beta, s0)
    o = rms_norm(o.astype(x.dtype), g_out) * jax.nn.silu(z.reshape(Bn, L, B_HEADS, B_VAL_DIM))
    out_b = o.reshape(Bn, L, B_WIDTH)

    x = x + jnp.concatenate([out_a, out_b], axis=-1) @ w_out.astype(x.dtype)

    h2 = rms_norm(x, g_ffn).reshape(Bn * L, D)
    x = x + hier_moe(h2, w_group, b_group, w_router, b_router, w_gate, w_up, w_down).reshape(Bn, L, D)

    gate = jax.nn.sigmoid(rms_norm(x, g_ple) @ w_ple_gate.astype(x.dtype))
    x = x + (p.astype(x.dtype) @ w_ple.astype(x.dtype)) * gate
    return x, new_buf, s_new.astype(x.dtype), v_a.reshape(Bn, L, A_WIDTH)

def setup_inputs(seed: int = 0) -> dict:
    key = jax.random.key(seed)
    ks = jax.random.split(key, 32)
    f32 = jnp.float32
    nrm = lambda k, shape, s: jax.random.normal(k, shape, f32) * s
    causal_mask = jnp.tril(jnp.ones((A_CHUNK, A_CHUNK), f32))
    return {
        "x_prompt": nrm(ks[0], (BATCH, SEQ, D_MODEL), 1.0),
        "x_sample": nrm(ks[1], (DEC_BATCH, DEC_SEQ, D_MODEL), 1.0),
        "state_conv": nrm(ks[2], (DEPTH, DEC_BATCH, CONV_W - 1, CONV_DIM), 1.0),
        "state_delta": nrm(ks[3], (DEPTH, DEC_BATCH, B_HEADS, B_KEY_DIM, B_VAL_DIM), 0.5),
        "p_prompt": nrm(ks[4], (DEPTH, BATCH, SEQ, PLE_DIM), 1.0),
        "p_sample": nrm(ks[5], (DEPTH, DEC_BATCH, DEC_SEQ, PLE_DIM), 1.0),
        "g_mix": 1.0 + nrm(ks[6], (DEPTH, D_MODEL), 0.02),
        "w_in": nrm(ks[7], (DEPTH, D_MODEL, IN_DIM), D_MODEL ** -0.5),
        "w_s": nrm(ks[8], (DEPTH, A_GROUPS, A_CHUNK, A_CHUNK), A_CHUNK ** -0.5) * causal_mask,
        "b_s": 1.0 + nrm(ks[9], (DEPTH, A_GROUPS, A_CHUNK), 0.02),
        "g_v": 1.0 + nrm(ks[10], (DEPTH, A_GROUPS, A_GROUP_DIM), 0.02),
        "conv_w": nrm(ks[11], (DEPTH, CONV_W, CONV_DIM), 0.5),
        "a_log": jnp.log(jax.random.uniform(ks[12], (DEPTH, B_HEADS), f32, 1.0, 16.0)),
        "dt_bias": nrm(ks[13], (DEPTH, B_HEADS), 0.1),
        "g_out": 1.0 + nrm(ks[14], (DEPTH, B_VAL_DIM), 0.02),
        "w_out": nrm(ks[15], (DEPTH, MIX_WIDTH, D_MODEL), MIX_WIDTH ** -0.5),
        "g_ffn": 1.0 + nrm(ks[16], (DEPTH, D_MODEL), 0.02),
        "w_group": nrm(ks[17], (DEPTH, D_MODEL, N_GROUPS), D_MODEL ** -0.5),
        "b_group": nrm(ks[18], (DEPTH, N_GROUPS), 0.01),
        "w_router": nrm(ks[19], (DEPTH, D_MODEL, N_EXPERTS), D_MODEL ** -0.5),
        "b_router": nrm(ks[20], (DEPTH, N_EXPERTS), 0.01),
        "w_gate": nrm(ks[21], (DEPTH, N_EXPERTS, D_MODEL, D_EXPERT), D_MODEL ** -0.5),
        "w_up": nrm(ks[22], (DEPTH, N_EXPERTS, D_MODEL, D_EXPERT), D_MODEL ** -0.5),
        "w_down": nrm(ks[23], (DEPTH, N_EXPERTS, D_EXPERT, D_MODEL), D_EXPERT ** -0.5),
        "g_ple": 1.0 + nrm(ks[24], (DEPTH, D_MODEL), 0.02),
        "w_ple_gate": nrm(ks[25], (DEPTH, D_MODEL, D_MODEL), D_MODEL ** -0.5),
        "w_ple": nrm(ks[26], (DEPTH, PLE_DIM, D_MODEL), PLE_DIM ** -0.5),
        "g_final": 1.0 + nrm(ks[27], (D_MODEL,), 0.02),
    }

def reference(x_prompt, x_sample, state_conv, state_delta, p_prompt, p_sample, g_mix, w_in, w_s, b_s, g_v,
              conv_w, a_log, dt_bias, g_out, w_out, g_ffn, w_group, b_group, w_router, b_router, w_gate, w_up,
              w_down, g_ple, w_ple_gate, w_ple, g_final):
    bp = x_prompt.shape[0]
    zero_conv = jnp.zeros((bp, CONV_W - 1, CONV_DIM), x_prompt.dtype)
    zero_delta = jnp.zeros((bp, B_HEADS, B_KEY_DIM, B_VAL_DIM), x_prompt.dtype)
    xp, xs = x_prompt, x_sample
    conv_p, delta_p, conv_s, delta_s, chunk_v_s = [], [], [], [], []
    for i in range(DEPTH):
        lw = (g_mix[i], w_in[i], w_s[i], b_s[i], g_v[i], conv_w[i], a_log[i], dt_bias[i], g_out[i], w_out[i],
              g_ffn[i], w_group[i], b_group[i], w_router[i], b_router[i], w_gate[i], w_up[i], w_down[i],
              g_ple[i], w_ple_gate[i], w_ple[i])
        xp, cb_p, sd_p, _ = hybrid_layer(xp, p_prompt[i], zero_conv, zero_delta, *lw)
        xs, cb_s, sd_s, va_s = hybrid_layer(xs, p_sample[i], state_conv[i], state_delta[i], *lw)
        conv_p.append(cb_p)
        delta_p.append(sd_p)
        conv_s.append(cb_s)
        delta_s.append(sd_s)
        chunk_v_s.append(va_s)
    y_prompt = rms_norm(xp, g_final)
    y_sample = rms_norm(xs, g_final)
    return (y_prompt, y_sample, jnp.stack(conv_p, 0), jnp.stack(delta_p, 0), jnp.stack(conv_s, 0),
            jnp.stack(delta_s, 0), jnp.stack(chunk_v_s, 0))


_drawn_inputs = setup_inputs


def setup_inputs(seed=0):
    import zlib

    import numpy as np

    out = dict(_drawn_inputs(seed))
    spreads = {}
    factors = {'b_s': 14.639,
     'g_v': 24.747,
     'dt_bias': 8.0,
     'g_out': 16.429,
     'b_group': 21.955,
     'b_router': 24.999,
     'g_ple': 200.0,
     'g_final': 22.059,
     'g_ffn': 3.177}
    for name, (base, spread) in spreads.items():
        noise = np.random.default_rng([zlib.crc32(name.encode()), seed]).standard_normal(out[name].shape)
        drawn = base * np.exp(spread * noise) if base else spread * noise
        out[name] = __import__('jax').numpy.asarray(drawn.astype(out[name].dtype))
    for name, factor in factors.items():
        out[name] = (out[name] * factor).astype(out[name].dtype)
    return out
```

```python
from contextlib import ExitStack

import numpy as np

import concourse.bass as bass
from concourse import mybir

F32 = mybir.dt.float32
I32 = mybir.dt.int32
ALU = mybir.AluOpType
ACT = mybir.ActivationFunctionType
AX = mybir.AxisListType.X

P = 128
D_MODEL = 2048
KT = D_MODEL // P
PROMPT = 256
SEQS, SEQ_LEN = 8, 4
SAMPLE = SEQS * SEQ_LEN
TOK = PROMPT + SAMPLE
TILES = ((0, 128), (128, 128), (256, SAMPLE))
HEADS = 8
WIDTH = 1024
CONV_DIM = 3 * WIDTH
TAPS = 4
PAD = TAPS - 1
SROW = PAD + SEQ_LEN
RAW = PAD + PROMPT + SEQS * SROW
S_AT = PAD + PROMPT
LEVELS = 7
EXPERTS, GROUPS, PER_GROUP = 32, 4, 8
D_EXP = 512
CAP = 64
PAIRS = EXPERTS // 2
MAX_ROUNDS = -(-TOK // CAP)
PLE = 256
EPS = 1e-6
SLOTS, SLOT = 12, 2048
PIECES = 6
Q, K, V, VA, U, Z = range(PIECES)
MOE_SLOT = 16 % SLOTS
RING_BASE = [(HEADS if s < PIECES else 0) + (2 if s < MOE_SLOT else 1) for s in range(SLOTS)]
TAIL_SLOTS = SLOTS - 2
V_CHAIN, A_CHAIN = 19, 4
FAR = 1e6

CONSTS = {}


def _constants():
    a = np.arange(P)
    row, col = a[:, None], a[None, :]
    same = (row // SEQ_LEN) == (col // SEQ_LEN)
    parts = [("ident", row == col), ("triu", row <= col), ("before", row < col), ("ones", row >= 0 * col),
             ("causal", row >= col), ("strict", row > col),
             ("low0", (row % 2 == 1) & (col == row - 1))]
    for lev in range(LEVELS):
        b = 1 << lev
        parts.append((f"mt{lev}", (col // b % 2 == 1) & (row // b == col // b - 1)))
    parts += [("iota", np.broadcast_to(np.arange(CAP)[None, :], (P, CAP))),
              ("iota99", np.broadcast_to(99 + np.arange(EXPERTS)[None, :], (P, EXPERTS))),
              ("rep", row == a[None, :SAMPLE] % SEQ_LEN),
              ("seq", row // SEQ_LEN == np.arange(SEQS)[None, :]),
              ("btriu", (same & (row <= col))[:, :SAMPLE]), ("ball", same[:, :SAMPLE]),
              ("bcausal", (same & (row >= col))[:, :SAMPLE]), ("bstrict", (same & (row > col))[:, :SAMPLE])]
    at = 0
    for name, m in parts:
        CONSTS[name] = (at, m.shape[1])
        at += m.shape[1]
    return np.concatenate([m.astype(np.float32) for _, m in parts], axis=1)


N_CONST = _constants().shape[1]

FILL = [3, 6, 6, 8] + [4, 4] * 6 + [5, 5, 5, 5, 5]
FILL.append(PIECES * KT - sum(FILL))
PIECE_AT = [next(n for n in range(len(FILL)) if sum(FILL[:n + 1]) >= KT * (s + 1)) for s in range(PIECES)]


def tail_slot(c):
    return (MOE_SLOT + c % TAIL_SLOTS) % SLOTS


class Chain:

    def __init__(self, eng, sem):
        self.eng, self.sem, self.n, self.base = eng, sem, 0, None

    def __call__(self, ins):
        ins.then_inc(self.sem, 1)
        self.n += 1

    def wait(self):
        self.eng.wait_ge(self.sem, self.n if self.base is None else self.base + self.n)


def trunk(nc, d, o):
    ctx = ExitStack()
    with ctx:
        def sb(name, shape, dt=F32):
            return ctx.enter_context(nc.sbuf_tensor(name, shape, dt))

        def sem(name):
            return ctx.enter_context(nc.semaphore(name))

        def sems(*names):
            return {n: sem(n) for n in names}

        cst = sb("cst", [P, N_CONST])
        x = sb("x", [P, 3, D_MODEL])
        hb = sb("hb", [P, 3 * D_MODEL])
        hn = hb[:, :].rearrange("p (t d) -> p t d", t=3)
        hT = sb("hT", [P, KT, TOK])
        mixT = sb("mixT", [P, KT, TOK])
        ring = sb("ring", [P, SLOTS * SLOT])
        ps = ctx.enter_context(nc.psum_tensor("ps", [P, 8, 512], F32))

        def C(name, rows=P, cols=None):
            at, n = CONSTS[name]
            return cst[0:rows, at:at + (cols or n)]

        def slot(s, **kw):
            v = ring[:, s * SLOT:(s + 1) * SLOT]
            return v

        class Carve:
            def __init__(self, *regions):
                self.regions = [[v, n, 0] for v, n in regions]

            def __call__(self, *shape):
                n = int(np.prod(shape))
                r = next(r for r in self.regions if r[2] + n <= r[1])
                v = r[0][:, r[2]:r[2] + n]
                r[2] += n
                if len(shape) == 2:
                    v = v.rearrange("p (a b) -> p a b", a=shape[0])
                elif len(shape) == 3:
                    v = v.rearrange("p (a b c) -> p a b c", a=shape[0], b=shape[1])
                return v

        grow = sb("grow", [3 * KT, P])
        gT = sb("gT", [P, 3, KT])
        gJ = sb("gJ", [P, KT])
        wab = sb("wab", [P, KT, 2 * HEADS])
        wr = sb("wr", [P, KT, GROUPS + EXPERTS])
        rbias = sb("rbias", [P, GROUPS + EXPERTS])
        goutT = sb("goutT", [P, 1])
        alog = sb("alog", [P, HEADS])
        dtb = sb("dtb", [P, HEADS])
        ss = sb("ss", [P, 3])
        rs2 = sb("rs2", [P, 3])
        cwr = sb("cwr", [TAPS * 3 * HEADS, P])
        cw = sb("cw", [P, TAPS, 3, HEADS])
        sc = sb("sc", [P, HEADS, 3, 5])
        hs = sb("hs", [P, 3, 5])
        hcw = sb("hcw", [P, TAPS, 3])
        ngexp = sb("ngexp", [P, HEADS])
        pre = sb("pre", [P, 8, 3, 8])
        ab = sb("ab", [P, 3, 16])

        more = sb("more", [P, 1152])
        w = Carve((ring[:, 6 * SLOT:12 * SLOT], 6 * SLOT), (hb[:, :], 3 * D_MODEL), (more[:, :], 1152))
        raw = w(3, RAW)
        raw_s = raw[:, :, S_AT:RAW].rearrange("p s (b c) -> p s b c", c=SROW)
        acc = w(3, RAW)
        acc_s = acc[:, :, S_AT:RAW].rearrange("p s (b c) -> p s b c", c=SROW)[:, :, :, 0:SEQ_LEN]
        qkvT = w(3, TOK)
        sq = w(2, TOK)
        rn = w(2, TOK)
        qk = w(2, TOK)
        gcol = w(3, P)
        dd = w(2, P)
        dds = w(SAMPLE)
        Dm = w(2, P)
        Ds = w(SAMPLE)
        DS = w(2, P)
        DSs = w(SAMPLE)
        eG = w(TOK)
        qg = w(TOK)
        Am = w(2, P)
        Ams = w(SAMPLE)
        QKm = w(2, P)
        QKms = w(SAMPLE)
        kbg = w(3, P)
        kd = w(3, P)
        vb = w(3, P)
        NT = w(LEVELS, 2, P)
        NTs = w(2, SAMPLE)
        QKT = w(2, P)
        QKTs = w(SAMPLE)
        X = w(2, P)
        XT = w(2, P)
        Xs = w(SAMPLE)
        XTs = w(SAMPLE)
        T1 = w(2, P)
        T1s = w(SAMPLE)
        us = w(2, P)
        wT = w(2, P)
        uTs = w(SAMPLE)
        WQ = w(SEQS, 2 * SEQ_LEN)
        S1 = w(P)
        S2 = w(P)
        vn1 = w(P)
        vnTs = w(SAMPLE)
        vns = w(P)
        Vm = w(SEQS, P)
        Sold = w(SEQS, P)
        Snew = w(SEQS, P)
        cs = w(3, PAD + SEQS * PAD)
        csT = w(3, P)
        stt = w(3, P)
        vaT = w(TOK)
        vd = w(3, P)
        vn = w(3, P)
        uT = w(TOK)
        zs = w(TOK)
        Wh = w(P)
        Wm = w(P)
        WT = w(P)
        WTs = w(SAMPLE)
        bB = w(P)
        gB = w(P)
        oS = w(TOK)
        osq, orn = rn[:, 0, :], rn[:, 1, :]
        ot = w(TOK)
        mA = ot
        DC = w(2, P)
        DCs = w(SAMPLE)
        lnj = Vm[:, 0:3, :]
        lnm, lns, lnr, lnq = (sb(n, [P, 3]) for n in ("lnm", "lns", "lnr", "lnq"))
        zero = sb("zero", [P, 1])
        eps = sb("eps", [P, 1])

        flat = mixT[:, :, :].rearrange("p k n -> p (k n)")
        junk = (flat[:, 0:D_MODEL], flat[:, D_MODEL:2 * D_MODEL],
                hT[:, :, :].rearrange("p k n -> p (k n)")[:, 0:D_MODEL])
        wd = Carve((flat[:, D_MODEL:], KT * TOK - D_MODEL))
        lg = wd(3, GROUPS + EXPERTS)
        rt = wd(9, 3, EXPERTS)
        rc = wd(12, 3)
        asg = sb("asg", [P, 3, EXPERTS])
        rankm = sb("rankm", [P, 3, EXPERTS + 2])
        wt = sb("wt", [P, 3, EXPERTS + 2])
        cnt = sb("cnt", [P, 1])
        rnd = sb("rnd", [P, MAX_ROUNDS])
        rnd_i = sb("rnd_i", [P, 1], I32)

        we = Carve((flat, KT * TOK), (hT[:, :, :].rearrange("p k n -> p (k n)"), KT * TOK))
        xg = we(D_MODEL)
        yx = we(D_MODEL)
        hx = we(2, 4, CAP)
        xT = we(KT, P)
        gu = we(2, D_EXP)
        sg = we(2, 4, CAP)
        Pm = we(3, 2 * CAP)
        WP = we(3, 2 * CAP)
        wpT = sb("wpT", [P, TOK])

        wf = Carve((flat, KT * TOK))
        sig = wf(4, 512)
        pin = more[:, 0:3 * PLE].rearrange("p (t n) -> p t n", t=3)
        pT = wf(2, TOK)
        smp = hb[:, 0:4 * 512].rearrange("p (g n) -> p g n", g=4)
        tmp = hb[:, 4 * 512:10 * 512].rearrange("p (g n) -> p g n", g=6)
        wp = ring[:, 2 * SLOT:4 * SLOT].rearrange("p (k n) -> p k n", k=2)
        gfin = ring[:, 4 * SLOT:5 * SLOT]

        ring_in = [sem(f"ring_in{s}") for s in range(SLOTS)]
        ld = sems("ld_const", "ld_x", "ld_small", "ld_route", "ld_conv")
        vec_chain, act_chain = sem("vec_chain"), sem("act_chain")
        outs = sem("outs")
        norm = sems("ss_zero", "rstd", "hnorm", "tile_T", "tile_out_v", "tile_out_a")
        dec = sems("prep_mm", "prep_v", "prep_a")
        E = sems("st_ld", "w_ld", "s0_ld", "st_T", "st_in", "vaT_T", "conv_r", "cs_r", "cs_T",
                 "cs_cp", "cs_st", "va_st", "s2_st", "sn_st", "qkv_r", "sq_r", "ss_mm", "qk_r", "tok_mm", "dd_r", "D_r",
                 "tok_cp", "A_r", "AT_mm", "QKT_r", "NT_r", "W_r", "dS_mm", "W_T", "WT_r", "Wrep", "WTs_r", "ln_d",
                 "ln_sq", "vn_r", "mixA_mm", "mixA_r", "uw_mm", "uw_cp", "WQ_r", "S1_mm", "S1_r", "SQ_mm", "wS_mm",
                 "vn1_r", "vnT_r", "vnTT", "Vm_r", "vns_r", "o_mm", "S2_r", "Sn_r", "os_p", "os_r", "osq_r", "oss_mm", "rn_r", "or_r",
                 "mixB_r")
        lev_mm, lev_cp, lev_x, lev_new = sem("lev_mm"), sem("lev_cp"), sem("lev_x"), sem("lev_new")
        piece_mm, piece_ev = sem("piece_mm"), sem("piece_ev")
        G = sems("out_mm", "out_used", "out_add", "smp_cp", "smp_add")
        R = sems("route_mm", "route_in", "route_exp", "asg_r", "rounds_r")
        M = sems("P_r", "WP_r", "wpt_T", "wpt_cp", "s0", "s1", "gT0", "gT1", "silu0", "silu1", "h0", "h1",
                 "gathA", "gathB", "rank_r", "xgA_v", "xgB_v", "xgA_a", "xgB_a", "y_v", "y_a", "xT_T", "xT_r",
                 "c0", "c1", "c2", "add0", "add1", "add2", "used", "moe_v")
        F = sems("p_in", "pT_T", "pT_r", "gate_used", "sig_r", "sigs_r", "ssum", "sg_r", "ssg_r", "pp_mm", "pp_r", "x_done", "y_r",
                 "gf_in", "wp_in")

        w_in = d["w_in"].rearrange("l (k p) n -> p (l k) n", p=P)
        conv_in = d["state_conv"].rearrange("l b r n -> (l b r) n")
        s_in = d["state_delta"].rearrange("l b h k v -> (l h) k b v")
        w_out = d["w_out"].rearrange("l (k p) n -> p (l k) n", p=P)
        w_pg = d["w_ple_gate"].rearrange("l (k p) n -> p (l k) n", p=P)
        w_gate = d["w_gate"].rearrange("l e (j p i) f -> (l e) j p (i f)", p=P, i=4)
        w_up = d["w_up"].rearrange("l e (j p i) f -> (l e) j p (i f)", p=P, i=4)
        w_down = d["w_down"].rearrange("l e (p i) n -> (l e) i p n", i=4)
        y_p, y_s, cv_p, sd_p, cv_s, sd_s, va_s = o
        y_p = y_p.rearrange("b (t p) n -> p (b t) n", p=P)
        y_s = y_s.rearrange("b l n -> (b l) n")
        cv_p = cv_p.rearrange("l b r n -> (l b r) n")
        cv_s = cv_s.rearrange("l b r n -> (l b r) n")
        sd_p = sd_p.rearrange("l b h k v -> (l b h) k v")
        sd_s = sd_s.rearrange("l b h k v -> (l h) k b v")
        va_s = va_s.rearrange("l b t n -> (l b t) n")
        piece_col = [2 * WIDTH, 3 * WIDTH, 4 * WIDTH, WIDTH, 0, 5 * WIDTH]

        block = ctx.enter_context(nc.Block())

        @block.sync
        def _(sp):
            sp.dma_start(cst[:], d["consts"]).then_inc(ld["ld_const"], 16)
            sp.dma_start(x[:, 0:2, :], d["x_prompt"].rearrange("b (t p) n -> p (b t) n", p=P)).then_inc(ld["ld_x"], 16)
            sp.dma_start(x[0:SAMPLE, 2, :], d["x_sample"].rearrange("b l n -> (b l) n")).then_inc(ld["ld_x"], 16)

            def load_piece(s, col):
                sp.dma_start(slot(s).rearrange("p (k n) -> p k n", k=KT),
                             w_in[:, :, bass.ds(col, P)]).then_inc(ring_in[s], 16)

            def load_state(cols):
                for s in range(3):
                    sp.dma_start(stt[0:SEQS * PAD, s, :], conv_in[:, bass.ds(cols[s], P)]).then_inc(E["st_ld"], 16)

            def load_gate(h):
                sp.dma_start(Wh, d["w_s"].rearrange("l h t s -> (l h) t s")[bass.ds(h, 1)].rearrange("a t s -> (a t) s")
                             ).then_inc(E["w_ld"], 16)
                sp.dma_start(bB, d["b_s"][0:1, bass.ds(h, 1), :].rearrange("a b t -> (a b) t").to_broadcast([P, P])
                             ).then_inc(E["w_ld"], 16)
                sp.dma_start(gB, d["g_v"][0:1, bass.ds(h, 1), :].rearrange("a b t -> (a b) t").to_broadcast([P, P])
                             ).then_inc(E["w_ld"], 16)

            def load_delta(h):
                sp.dma_start(Sold, s_in[bass.ds(h, 1)].rearrange("a k b v -> (a k) b v")).then_inc(E["s0_ld"], 16)

            for s in range(PIECES):
                load_piece(s, piece_col[s])
            sp.wait_ge(norm["tile_T"], KT)
            load_state([s * WIDTH for s in range(3)])
            load_gate(0)
            load_delta(0)
            for s in range(PIECES):
                sp.wait_ge(piece_mm, s + 1)
                load_piece(s, P + piece_col[s])

            def head(h, pieces, inputs):
                snap = (lambda v: v) if isinstance(h, int) else sp.snap
                c = [snap(h * P + s * WIDTH) for s in range(3)]
                c1 = [snap(h * P + (P + s * WIDTH)) for s in range(3)]
                h1, h2, hn_ = snap(h + 1), snap(h + 2), snap(h + 1)

                def piece(s):
                    if pieces:
                        at = snap(h * PIECES + (PIECES + s + 1))
                        col = snap(h * P + (2 * P + piece_col[s]))
                        sp.wait_ge(piece_mm, at)
                        load_piece(s, col)
                if inputs:
                    sp.wait_ge(E["st_in"], h1)
                    load_state(c1)
                sp.wait_ge(norm["tile_T"], KT)
                sp.wait_ge(E["cs_cp"], h1)
                for s in range(3):
                    sp.dma_start(cv_p[:, bass.ds(c[s], P)], csT[0:PAD, s, :]).then_inc(E["cs_st"], 16)
                    sp.dma_start(cv_s[:, bass.ds(c[s], P)], csT[PAD:PAD + SEQS * PAD, s, :]).then_inc(E["cs_st"], 16)
                piece(Q)
                piece(K)
                sp.wait_ge(E["vn_r"], h1)
                sp.dma_start(va_s[:, bass.ds(c[0], P)], vn[0:SAMPLE, 2, :]).then_inc(E["va_st"], 16)
                piece(V)
                if inputs:
                    sp.wait_ge(E["mixA_r"], h1)
                    load_gate(hn_)
                piece(VA)
                sp.wait_ge(E["S2_r"], h1)
                sp.dma_start(sd_p[bass.ds(h, 1)].rearrange("a k v -> (a k) v"), S2).then_inc(E["s2_st"], 16)
                piece(U)
                sp.wait_ge(E["Sn_r"], h1)
                sp.dma_start(sd_s[bass.ds(h, 1)].rearrange("a k b v -> (a k) b v"), Snew).then_inc(E["sn_st"], 16)
                if inputs:
                    load_delta(hn_)
                piece(Z)

            with sp.Fori(0, HEADS - 2) as h:
                head(h, True, True)
            head(HEADS - 2, False, True)
            head(HEADS - 1, False, False)

            for c in range(16):
                half, kk = divmod(c, 8)
                s = c % SLOTS
                if c < PIECES:
                    sp.wait_ge(piece_mm, (HEADS - 1) * PIECES + c + 1)
                elif c < SLOTS:
                    sp.wait_ge(E["mixB_r"], HEADS)
                    sp.wait_ge(E["cs_st"], 6 * 16 * HEADS)
                    sp.wait_ge(E["va_st"], 16 * HEADS)
                    sp.wait_ge(E["s2_st"], 16 * HEADS)
                    sp.wait_ge(E["sn_st"], 16 * HEADS)
                else:
                    sp.wait_ge(G["out_used"], c - SLOTS + 1)
                sp.dma_start(slot(s).rearrange("p (k n) -> p k n", k=2),
                             w_out[:, 2 * kk:2 * kk + 2, half * 1024:(half + 1) * 1024]).then_inc(ring_in[s], 16)

            def expert_of(c):
                return c // 8 if c < 16 else (c - 16) % 2

            def expert_chunk(c, e):
                r = c % 8 if c < 16 else (c - 16) // 2
                if c < 16:
                    src = (w_gate, w_up)[r % 2][bass.ds(e, 1), r // 2]
                else:
                    src = w_down[bass.ds(e, 1), r]
                s = (MOE_SLOT + c) % SLOTS
                sp.dma_start(slot(s), src.rearrange("a p n -> (a p) n")).then_inc(ring_in[s], 16)

            def gate_chunk(c):
                half, kk = divmod(c, 8)
                sp.dma_start(slot(tail_slot(c)).rearrange("p (k n) -> p k n", k=2),
                             w_pg[:, 2 * kk:2 * kk + 2, half * 1024:(half + 1) * 1024]).then_inc(ring_in[tail_slot(c)], 16)

            for c in range(SLOTS):
                sp.wait_ge(G["out_used"], c + 16 - SLOTS + 1)
                expert_chunk(c, expert_of(c))
            sp.wait_ge(R["rounds_r"], 1)
            rounds = sp.value_load(rnd_i[0:1, 0:1], min_val=1, max_val=MAX_ROUNDS)
            with sp.Fori(0, rounds) as r:
                with sp.Fori(0, PAIRS - 1) as it:
                    for c in range(24):
                        e = sp.snap(it * 2 + ((0 if c < 12 else 2) + expert_of((c + 12) % 24)))
                        first_down = 16 - 12
                        if c != first_down + 1:
                            k = sp.snap(r * (24 * PAIRS) + it * 24 + (c + (2 if c == first_down else 1)))
                            sp.wait_ge(M["used"], k)
                        expert_chunk((c + 12) % 24, e)
                for c in range(SLOTS):
                    k = sp.snap(r * (24 * PAIRS) + (24 * (PAIRS - 1) + c + 1))
                    sp.wait_ge(M["used"], k)
                    expert_chunk(c + 12, EXPERTS - 2 + expert_of(c + 12))
                k = [sp.snap(r * (24 * PAIRS) + (24 * (PAIRS - 1) + 12 + c + 1)) for c in range(SLOTS)]
                with sp.If(sp.snap(r + 1) < rounds):
                    for c in range(SLOTS):
                        sp.wait_ge(M["used"], k[c])
                        expert_chunk(c, expert_of(c))
                with sp.Else():
                    for c in range(TAIL_SLOTS):
                        sp.wait_ge(M["used"], k[c])
                        gate_chunk(c)
                    sp.wait_ge(M["used"], k[SLOTS - 1])
                    sp.dma_start(wp[:, :, :], d["w_ple"].rearrange("l (k p) n -> p (l k) n", p=P)).then_inc(F["wp_in"], 16)

            for c in range(TAIL_SLOTS, 16):
                sp.wait_ge(F["gate_used"], c - TAIL_SLOTS + 1)
                gate_chunk(c)
            for n in range(3):
                sp.wait_ge(F["y_r"], n + 1)
                if n < 2:
                    sp.dma_start(y_p[:, n, :], x[:, n, :]).then_inc(outs, 16)
                else:
                    sp.dma_start(y_s, x[0:SAMPLE, 2, :]).then_inc(outs, 16)
            sp.wait_ge(outs, 48)

        @block.tensor
        def _(pe):
            def mm(out, lhsT, rhs, start=True, stop=True):
                return pe.matmul(out, lhsT, rhs, start=start, stop=stop)

            def tr(out, in_, n):
                return pe.transpose(out, in_, C("ident", n, n))

            def tile_transposes(ph):
                pe.wait_ge(norm["hnorm"], 3 * (ph + 1))
                for k in range(KT):
                    if k >= 8:
                        pe.wait_ge(norm["tile_out_a" if k % 2 else "tile_out_v"], 8 * ph + (k - 8) // 2 + 1)
                    for t, (off, n) in enumerate(TILES):
                        last = tr(ps[:, k % 8, off:off + n], hn[0:n, t, k * P:(k + 1) * P], n)
                    last.then_inc(norm["tile_T"], 1)
                pe.wait_ge(norm["tile_out_v"], 8 * (ph + 1))
                pe.wait_ge(norm["tile_out_a"], 8 * (ph + 1))

            pe.wait_ge(ld["ld_const"], 16)
            pe.wait_ge(ld["ld_conv"], 16 * 4)
            tr(ps[:, 7, 0:96], cwr[:, :], 96)
            tr(ps[:, 7, 96:96 + 3 * KT], grow[:, :], 3 * KT).then_inc(dec["prep_mm"], 1)
            pe.wait_ge(dec["prep_v"], 1)
            tile_transposes(0)
            pe.wait_ge(ld["ld_small"], 16 * 4)
            for t, (off, n) in enumerate(TILES):
                for k in range(KT):
                    last = mm(ps[0:n, 2, t * 16:(t + 1) * 16], hT[:, k, off:off + n], wab[:, k, :], k == 0, k == KT - 1)
            last.then_inc(dec["prep_mm"], 1)

            class Projection:

                def __init__(self, g, in_value, this, before):
                    self.at, self.in_value, self.this, self.before = 0, in_value, this, before

                def go(self, n):
                    for _ in range(n):
                        s, k = divmod(self.at, KT)
                        self.at += 1
                        if k == 0:
                            pe.wait_ge(ring_in[s], self.in_value)
                            if s >= 2 or self.before:
                                pe.wait_ge(piece_ev, self.this(s - 2))
                        last = mm(ps[:, s % 2, 0:TOK], slot(s)[:, k * P:(k + 1) * P], hT[:, k, :], k == 0, k == KT - 1)
                        if k == KT - 1:
                            last.then_inc(piece_mm, 1)

            Projection(0, 16, lambda s: s + 1, False).go(PIECES * KT)

            pe.wait_ge(dec["prep_v"], 3)
            g = pre[:, 0]
            for t in range(2):
                mm(ps[:, 3, t * 8:t * 8 + 8], C("triu"), g[:, t, :])
                mm(ps[:, 3, 24 + t * 8:32 + t * 8], C("ones"), g[:, t, :])
            mm(ps[0:SAMPLE, 3, 16:24], C("btriu", SAMPLE), g[0:SAMPLE, 2, :])
            mm(ps[0:SAMPLE, 3, 40:48], C("ball", SAMPLE), g[0:SAMPLE, 2, :]).then_inc(dec["prep_mm"], 1)

            def head(h, fill):
                snap = (lambda v: v) if isinstance(h, int) else pe.snap
                h1, h0 = snap(h + 1), snap(h + 0)
                gemm = Projection(h, snap((h + 2) * 16), lambda s: snap(h * PIECES + (PIECES + s + 1)), True) if fill else None
                step = [0]

                def next_head():
                    if fill:
                        gemm.go(FILL[step[0]])
                    step[0] += 1

                pe.wait_ge(piece_ev, snap(h * PIECES + (VA + 1)))
                pe.wait_ge(E["st_ld"], snap((h + 1) * 48))
                pe.wait_ge(E["mixB_r"], h0)
                pe.wait_ge(E["Sn_r"], h0)
                for t, (off, n) in enumerate(TILES):
                    last = pe.transpose(ps[0:n, 3, t * P:(t + 1) * P], vaT[:, off:off + n], C("ident"))
                last.then_inc(E["vaT_T"], 1)
                for s in range(3):
                    last = tr(ps[:, 2, s * 24:(s + 1) * 24], stt[0:SEQS * PAD, s, :], SEQS * PAD)
                last.then_inc(E["st_T"], 1)
                pe.wait_ge(E["cs_r"], h1)
                for s in range(3):
                    last = tr(ps[0:27, 4, s * P:(s + 1) * P], cs[:, s, :], P)
                last.then_inc(E["cs_T"], 1)
                next_head()
                pe.wait_ge(E["sq_r"], h1)
                pe.wait_ge(E["st_in"], h1)
                pe.wait_ge(E["cs_cp"], h1)
                mm(ps[:, 2, 0:TOK], C("ones"), sq[:, 0, :])
                mm(ps[:, 4, 0:TOK], C("ones"), sq[:, 1, :]).then_inc(E["ss_mm"], 1)
                next_head()
                pe.wait_ge(E["qk_r"], h1)
                for t, (off, n) in enumerate(TILES):
                    pe.transpose(ps[0:n, 5, t * P:(t + 1) * P], qk[:, 1, off:off + n], C("ident"))
                    pe.transpose(ps[0:n, 6, t * P:(t + 1) * P], qkvT[:, 2, off:off + n], C("ident"))
                for t in range(2):
                    kt, qt = qk[:, 1, t * P:(t + 1) * P], qk[:, 0, t * P:(t + 1) * P]
                    mm(ps[:, 7, t * P:(t + 1) * P], kt, kt)
                    mm(ps[:, 7, 256 + t * P:256 + (t + 1) * P], qt, kt)
                    mm(ps[:, 2, t * P:(t + 1) * P], gcol[:, t, :], C("triu"))
                kt, qt = qk[:, 1, PROMPT:TOK], qk[:, 0, PROMPT:TOK]
                mm(ps[0:SAMPLE, 4, 0:SAMPLE], kt, kt)
                mm(ps[0:SAMPLE, 4, SAMPLE:2 * SAMPLE], qt, kt)
                mm(ps[:, 2, PROMPT:TOK], gcol[0:SAMPLE, 2, :], C("btriu", SAMPLE)).then_inc(E["tok_mm"], 1)
                next_head()
                pe.wait_ge(E["A_r"], h1)
                pe.wait_ge(E["tok_cp"], h1)
                pe.wait_ge(E["D_r"], h1)
                for t in range(2):
                    tr(ps[:, 5, t * P:(t + 1) * P], Am[:, t, :], P)
                    tr(ps[:, 6, t * P:(t + 1) * P], QKm[:, t, :], P)
                tr(ps[0:SAMPLE, 5, 256:256 + SAMPLE], Ams[0:SAMPLE, :], SAMPLE)
                tr(ps[0:SAMPLE, 6, 256:256 + SAMPLE], QKms[0:SAMPLE, :], SAMPLE).then_inc(E["AT_mm"], 1)
                next_head()
                for lev in range(1, LEVELS):
                    base = (LEVELS - 1)
                    v = snap(h * base + lev)
                    if lev == 1:
                        pe.wait_ge(E["NT_r"], h1)
                    else:
                        pe.wait_ge(lev_new, snap(h * base + lev - 1))
                    for t in range(2):
                        last = mm(ps[:, 5, t * P:(t + 1) * P], NT[:, lev, t, :], X[:, t, :])
                    if lev == 1:
                        last = mm(ps[0:SAMPLE, 5, 256:256 + SAMPLE], NTs[0:SAMPLE, 1, :], Xs[0:SAMPLE, :])
                    last.then_inc(lev_mm, 1)
                    next_head()
                    pe.wait_ge(lev_cp, v)
                    if lev == 1:
                        pe.wait_ge(E["QKT_r"], h1)
                    for t in range(2):
                        if lev < LEVELS - 1:
                            mm(ps[:, 6, t * P:(t + 1) * P], XT[:, t, :], T1[:, t, :])
                        last = mm(ps[:, 7, t * P:(t + 1) * P], T1[:, t, :], XT[:, t, :])
                    if lev == 1:
                        last = mm(ps[0:SAMPLE, 7, 256:256 + SAMPLE], T1s[0:SAMPLE, :], XTs[0:SAMPLE, :])
                    last.then_inc(lev_x, 1)
                    if lev == 2:
                        pe.wait_ge(E["W_r"], h1)
                        tr(ps[:, 2, 0:P], Wm, P).then_inc(E["W_T"], 1)
                    if lev == 3:
                        pe.wait_ge(E["WT_r"], h1)
                        mm(ps[0:SAMPLE, 3, 0:SEQ_LEN], C("rep"), WT[:, 0:SEQ_LEN]).then_inc(E["Wrep"], 1)
                    if lev == 5:
                        pe.wait_ge(E["WTs_r"], h1)
                        pe.wait_ge(E["vn_r"], h1)
                        for t in range(2):
                            mm(ps[:, 4, t * P:(t + 1) * P], vn[:, t, :], WT)
                        mm(ps[:, 4, PROMPT:TOK], vn[0:SAMPLE, 2, :], WTs[0:SAMPLE, :]).then_inc(E["mixA_mm"], 1)
                    next_head()
                pe.wait_ge(lev_new, snap((h + 1) * (LEVELS - 1)))
                for t in range(2):
                    mm(ps[:, 5, t * P:(t + 1) * P], XT[:, t, :], vb[:, t, :])
                    mm(ps[:, 6, t * P:(t + 1) * P], kbg[:, t, :], XT[:, t, :])
                mm(ps[:, 5, PROMPT:TOK], vb[0:SAMPLE, 2, :], XTs[0:SAMPLE, :])
                mm(ps[:, 6, PROMPT:TOK], kbg[0:SAMPLE, 2, :], XTs[0:SAMPLE, :]).then_inc(E["uw_mm"], 1)
                next_head()
                pe.wait_ge(E["uw_cp"], h1)
                pe.wait_ge(E["mixA_r"], h1)
                mm(ps[:, 7, 0:P], kd[:, 0, :], us[:, 0, :]).then_inc(E["S1_mm"], 1)
                mm(ps[:, 4, 0:P], us[:, 0, :], QKT[:, 0, :])
                pe.wait_ge(E["s0_ld"], snap((h + 1) * 16))
                pe.wait_ge(E["WQ_r"], h1)
                for b in range(SEQS):
                    last = mm(ps[:, 2, b * 8:(b + 1) * 8], Sold[:, b, :], WQ[:, b, :])
                last.then_inc(E["SQ_mm"], 1)
                next_head()
                pe.wait_ge(E["S1_r"], h1)
                mm(ps[:, 3, 0:P], wT[:, 1, :], S1).then_inc(E["wS_mm"], 1)
                pe.wait_ge(E["vnT_r"], h1)
                pe.transpose(ps[0:SAMPLE, 5, 0:P], vnTs, C("ident")).then_inc(E["vnTT"], 1)
                next_head()
                pe.wait_ge(E["vn1_r"], h1)
                mm(ps[:, 4, P:2 * P], S1, qg[:, P:2 * P], True, False)
                mm(ps[:, 4, P:2 * P], vn1, QKT[:, 1, :], False, True)
                mm(ps[:, 7, P:2 * P], kd[:, 1, :], vn1)
                pe.wait_ge(E["vns_r"], h1)
                mm(ps[:, 4, PROMPT:TOK], vns[0:SAMPLE, :], QKTs[0:SAMPLE, :]).then_inc(E["o_mm"], 1)
                next_head()
                pe.wait_ge(E["Vm_r"], h1)
                for q in range(2):
                    last = mm(ps[:, 5 + q, :], kd[0:SAMPLE, 2, :], Vm[0:SAMPLE, 4 * q:4 * q + 4, :])
                last.then_inc(E["dS_mm"], 1)
                pe.wait_ge(E["osq_r"], h1)
                mm(ps[:, 3, 0:TOK], C("ones"), osq).then_inc(E["oss_mm"], 1)
                next_head()
                next_head()

            pe.wait_ge(dec["prep_v"], 4)
            with pe.Fori(0, HEADS - 1) as h:
                head(h, True)
            head(HEADS - 1, False)

            def dense(src, in_sem, in_value, used, slot_of, half):
                for kk in range(8):
                    c = half * 8 + kk
                    s = slot_of(c)
                    pe.wait_ge(in_sem[s], in_value(c))
                    wv = slot(s).rearrange("p (k n) -> p k n", k=2)
                    for kp in range(2):
                        k = 2 * kk + kp
                        for t in range(2):
                            for n in range(2):
                                mm(ps[:, 2 * t + n, :], src[:, k, t * P:(t + 1) * P], wv[:, kp, n * 512:(n + 1) * 512],
                                   k == 0, k == KT - 1)
                    for kp in range(2):
                        for n in range(2):
                            g = 2 * kp + n
                            last = mm(ps[32 * g:32 * g + 32, 4, :], src[:, 2 * kk + kp, PROMPT:TOK],
                                      wv[:, kp, n * 512:(n + 1) * 512], kk == 0, kk == 7)
                    last.then_inc(used, 1)

            pe.wait_ge(E["mixB_r"], HEADS)
            pe.wait_ge(E["Sn_r"], HEADS)
            for half in range(2):
                if half:
                    pe.wait_ge(G["out_add"], 1)
                    pe.wait_ge(G["smp_cp"], 1)
                dense(mixT, ring_in, lambda c: 16 * (HEADS + 1 + c // SLOTS) if c % SLOTS < PIECES else 16 * (1 + c // SLOTS),
                      G["out_used"], lambda c: c % SLOTS, half)

            pe.wait_ge(G["out_add"], 2)
            pe.wait_ge(G["smp_add"], 2)
            tile_transposes(1)
            pe.wait_ge(ld["ld_route"], 16 * 5)
            for t, (off, n) in enumerate(TILES):
                for k in range(KT):
                    last = mm(ps[0:n, 0, t * 36:(t + 1) * 36], hT[:, k, off:off + n], wr[:, k, :], k == 0, k == KT - 1)
            last.then_inc(R["route_mm"], 1)
            pe.wait_ge(R["asg_r"], 1)
            a0, a1, a2 = asg[:, 0, :], asg[:, 1, :], asg[0:SAMPLE, 2, :]
            mm(ps[:, 1, 0:32], C("before"), a0)
            mm(ps[:, 1, 32:64], C("ones"), a0, True, False)
            mm(ps[:, 1, 32:64], C("before"), a1, False, True)
            mm(ps[0:SAMPLE, 1, 64:96], C("ones", P, SAMPLE), a0, True, False)
            mm(ps[0:SAMPLE, 1, 64:96], C("ones", P, SAMPLE), a1, False, False)
            mm(ps[0:SAMPLE, 1, 64:96], C("before", SAMPLE, SAMPLE), a2, False, True)
            mm(ps[:, 1, 96:128], C("ones"), a0, True, False)
            mm(ps[:, 1, 96:128], C("ones"), a1, False, False)
            mm(ps[:, 1, 96:128], C("ones", SAMPLE), a2, False, True).then_inc(R["route_mm"], 1)

            pe.wait_ge(R["rounds_r"], 1)
            rounds = pe.value_load(rnd_i[0:1, 0:1], min_val=1, max_val=MAX_ROUNDS)

            def gather(nn, banks):
                for n in nn:
                    for t, (off, m) in enumerate(TILES):
                        last = mm(ps[:, banks[n], :], Pm[0:m, t, :], hn[0:m, t, n * 512:(n + 1) * 512], t == 0, t == 2)
                return last

            def expert_inputs(v_a, v_v):
                pe.wait_ge(M["xgB_v"], v_v)
                pe.wait_ge(M["xgB_a"], v_a)
                for j in range(4):
                    xv = xg[:, j * 512:(j + 1) * 512].rearrange("s (q i) -> s i q", i=4)
                    for i in range(4):
                        last = tr(ps[:, 4 + j, i * P:(i + 1) * P], xv[:, i, :], P)
                last.then_inc(M["xT_T"], 1)

            BANK = (0, 1, 6, 7)
            with pe.Fori(0, rounds) as r:
                q1 = pe.snap(r * (PAIRS + 1) + 1)
                n0 = pe.snap(r * PAIRS)
                pe.wait_ge(M["add2"], n0)
                pe.wait_ge(M["add1"], n0)
                pe.wait_ge(M["P_r"], q1)
                gather((0, 1), BANK).then_inc(M["gathA"], 1)
                gather((2, 3), BANK).then_inc(M["gathB"], 1)
                expert_inputs(q1, q1)
                with pe.Fori(0, PAIRS) as it:
                    n0 = pe.snap(r * PAIRS + it)
                    n1 = pe.snap(n0 + 1)
                    q1 = pe.snap(r * (PAIRS + 1) + it + 1)
                    q2 = pe.snap(q1 + 1)
                    in1 = pe.snap((n0 * 2 + 1) * 16)
                    in2 = pe.snap((n0 * 2 + 2) * 16)

                    def landed(c):
                        s = (MOE_SLOT + c) % SLOTS
                        b = RING_BASE[s] * 16
                        return ring_in[s], (moe_v[b, c // SLOTS])

                    moe_v = {(b, q): pe.snap((in1, in2)[q] + b) for b in sorted({16 * v for v in RING_BASE}) for q in range(2)}
                    pe.wait_ge(M["WP_r"], q1)
                    pe.wait_ge(M["add2"], n0)
                    for t, (off, m) in enumerate(TILES):
                        last = pe.transpose(ps[:, 2, off:off + m], WP[0:m, t, :], C("ident", m, m))
                    last.then_inc(M["wpt_T"], 1)
                    pe.wait_ge(M["xT_r"], q1)
                    for ex in range(2):
                        for j in range(4):
                            for u in range(2):
                                sm, v = landed(8 * ex + 2 * j + u)
                                pe.wait_ge(sm, v)
                            for i in range(4):
                                k = 4 * j + i
                                for u in range(2):
                                    s = (MOE_SLOT + 8 * ex + 2 * j + u) % SLOTS
                                    last = mm(ps[64 * u:64 * u + 64, 4 + ex, :], xT[:, k, ex * CAP:(ex + 1) * CAP],
                                              slot(s)[:, i * 512:(i + 1) * 512], k == 0, k == KT - 1)
                                    if i == 3:
                                        last.then_inc(M["used"], 1)
                    pe.wait_ge(M["s0"], n1)
                    pe.wait_ge(M["wpt_cp"], n1)
                    for i in range(4):
                        last = tr(ps[:, 2, i * P:(i + 1) * P], gu[:, 0, :].rearrange("s (q i) -> s i q", i=4)[:, i, :], P)
                    last.then_inc(M["gT0"], 1)
                    pe.wait_ge(M["P_r"], q2)
                    gather((0, 1), BANK).then_inc(M["gathA"], 1)
                    pe.wait_ge(M["s1"], n1)
                    for i in range(4):
                        last = tr(ps[:, 3, i * P:(i + 1) * P], gu[:, 1, :].rearrange("s (q i) -> s i q", i=4)[:, i, :], P)
                    last.then_inc(M["gT1"], 1)
                    gather((2, 3), BANK).then_inc(M["gathB"], 1)
                    pe.wait_ge(M["xgA_v"], q2)
                    pe.wait_ge(M["xgA_a"], q2)
                    pe.wait_ge(M["h0"], n1)
                    pe.wait_ge(M["h1"], n1)
                    for i in range(4):
                        for ex in range(2):
                            sm, v = landed(16 + 2 * i + ex)
                            pe.wait_ge(sm, v)
                        for n in range(4):
                            for ex in range(2):
                                s = (MOE_SLOT + 16 + 2 * i + ex) % SLOTS
                                last = mm(ps[64 * ex:64 * ex + 64, n, :], hx[:, ex, i, :], slot(s)[:, n * 512:(n + 1) * 512],
                                          i == 0, i == 3)
                                if n == 3:
                                    last.then_inc(M["used"], 1)
                    expert_inputs(q2, q2)
                    pe.wait_ge(M["y_v"], n1)
                    pe.wait_ge(M["y_a"], n1)
                    for t, (off, m) in enumerate(TILES):
                        if t == 1:
                            pe.wait_ge(M["xT_r"], q2)
                        if t == 2:
                            pe.wait_ge(M["add0"], n1)
                        for n in range(4):
                            last = mm(ps[0:m, (t % 2) * 4 + n, :], wpT[:, off:off + m], yx[:, n * 512:(n + 1) * 512])
                        last.then_inc(M[f"c{t}"], 1)

            pe.wait_ge(M["moe_v"], 1)
            tile_transposes(2)
            pe.wait_ge(F["p_in"], 32)
            for t, (off, n) in enumerate(TILES):
                for k in range(2):
                    last = tr(ps[:, k, off:off + n], pin[0:n, t, k * P:(k + 1) * P], n)
            last.then_inc(F["pT_T"], 1)
            pe.wait_ge(F["wp_in"], 16)
            pe.wait_ge(F["pT_r"], 1)
            for half in range(2):
                if half:
                    pe.wait_ge(F["sig_r"], 4)
                    pe.wait_ge(F["sigs_r"], 1)
                dense(hT, ring_in, lambda c: pe.snap(rounds * (2 * PAIRS * 16) + 16 * (RING_BASE[tail_slot(c)] + 1 + c // TAIL_SLOTS)),
                      F["gate_used"], tail_slot, half)
                for n in range(2):
                    for t in range(2):
                        q = half * 6 + n * 3 + t
                        if q >= 3:
                            pe.wait_ge(F["pp_r"], q - 2)
                        for k in range(2):
                            last = mm(ps[:, 5 + t, :], pT[:, k, t * P:(t + 1) * P],
                                      wp[:, k, half * 1024 + n * 512:half * 1024 + (n + 1) * 512], k == 0, k == 1)
                        last.then_inc(F["pp_mm"], 1)
                    q = half * 6 + n * 3 + 2
                    if q >= 3:
                        pe.wait_ge(F["pp_r"], q - 2)
                    for k in range(2):
                        last = mm(ps[0:SAMPLE, 7, :], pT[:, k, PROMPT:TOK],
                                  wp[:, k, half * 1024 + n * 512:half * 1024 + (n + 1) * 512], k == 0, k == 1)
                    last.then_inc(F["pp_mm"], 1)

        @block.scalar
        def _(act):
            def f(out, in_, func=ACT.Copy, **kw):
                return act.activation(out, in_, func, **kw)

            for dst, src in ((cwr[:, :], d["conv_w"].rearrange("l w (t p) -> (l w t) p", p=P)),
                             (grow[0:KT, :], d["g_mix"].rearrange("l (k p) -> (l k) p", p=P)),
                             (grow[KT:2 * KT, :], d["g_ffn"].rearrange("l (k p) -> (l k) p", p=P)),
                             (grow[2 * KT:3 * KT, :], d["g_ple"].rearrange("l (k p) -> (l k) p", p=P))):
                act.dma_start(dst, src).then_inc(ld["ld_conv"], 16)
            act.dma_start(wab[:, :, :], w_in[:, :, 6 * WIDTH:6 * WIDTH + 2 * HEADS]).then_inc(ld["ld_small"], 16)
            act.dma_start(alog[:, :], d["a_log"].to_broadcast([P, HEADS])).then_inc(ld["ld_small"], 16)
            act.dma_start(dtb[:, :], d["dt_bias"].to_broadcast([P, HEADS])).then_inc(ld["ld_small"], 16)
            act.dma_start(goutT[:, :], d["g_out"].rearrange("l (p a) -> p (l a)", a=1)).then_inc(ld["ld_small"], 16)
            act.dma_start(gJ[:, :].rearrange("p (j i) -> p j i", i=4),
                          d["g_ffn"].rearrange("l (j p i) -> p (l j) i", p=P, i=4)).then_inc(ld["ld_route"], 16)
            act.dma_start(wr[:, :, 0:GROUPS], d["w_group"].rearrange("l (k p) e -> p (l k) e", p=P)).then_inc(ld["ld_route"], 16)
            act.dma_start(wr[:, :, GROUPS:], d["w_router"].rearrange("l (k p) e -> p (l k) e", p=P)).then_inc(ld["ld_route"], 16)
            act.dma_start(rbias[:, 0:GROUPS], d["b_group"].to_broadcast([P, GROUPS])).then_inc(ld["ld_route"], 16)
            act.dma_start(rbias[:, GROUPS:], d["b_router"].to_broadcast([P, EXPERTS])).then_inc(ld["ld_route"], 16)

            ac = Chain(act, act_chain)

            def rstd(pairs, n, signal, func=None):
                for out, in_, rows in pairs:
                    last = f(out, in_, ACT.Ln, scale=1.0 / n, bias=eps[0:rows, :])
                ac(last)
                ac.wait()
                for out, _, _ in pairs:
                    last = f(out, out, ACT.Exp, scale=-0.5)
                last.then_inc(signal, 1)

            def rms():
                for t, (_, n) in enumerate(TILES):
                    last = f(junk[t][0:n, :], x[0:n, t, :], ACT.Square, accum_out=ss[0:n, t:t + 1])
                ac(last)
                ac.wait()
                rstd([(rs2[:, :], ss[:, :], P)], D_MODEL, norm["rstd"])

            def tiles_out(ph):
                for k in range(1, KT, 2):
                    act.wait_ge(norm["tile_T"], KT * ph + k + 1)
                    f(hT[:, k, :], ps[:, k % 8, 0:TOK], scale=gT[:, ph, k:k + 1]).then_inc(norm["tile_out_a"], 1)

            act.wait_ge(norm["ss_zero"], 1)
            act.wait_ge(ld["ld_x"], 32)
            rms()
            act.wait_ge(dec["prep_v"], 1)
            tiles_out(0)
            act.wait_ge(ld["ld_small"], 16 * 4)
            act.wait_ge(dec["prep_v"], 2)
            f(ngexp[:, :], alog[:, :], ACT.Exp)
            f(pre[:, 4], ab[:, :, HEADS:], ACT.Exp, scale=-1.0)
            f(pre[:, 3], pre[:, 2], ACT.Exp, scale=-1.0).then_inc(dec["prep_a"], 1)
            act.wait_ge(dec["prep_a"], 1)
            f(pre[:, 7], pre[:, 3], ACT.Ln, bias=1.0).then_inc(dec["prep_a"], 1)

            def piece_out(s, this, before):
                bank = ps[:, s % 2, :]
                act.wait_ge(piece_mm, this)
                if s <= V:
                    if before is not None:
                        act.wait_ge(E["cs_r"], before)
                        act.wait_ge(E["conv_r"], before)
                    f(raw[:, s, PAD:S_AT], bank[:, 0:PROMPT])
                    last = f(raw[:, s, S_AT:RAW].rearrange("p (b c) -> p b c", c=SROW)[:, :, PAD:],
                             bank[:, PROMPT:TOK].rearrange("p (b c) -> p b c", c=SEQ_LEN))
                elif s == VA:
                    if before is not None:
                        act.wait_ge(E["vaT_T"], before)
                    last = f(vaT, bank[:, 0:TOK], ACT.Gelu_apprx_tanh)
                elif s == U:
                    if before is not None:
                        act.wait_ge(E["mixA_r"], before)
                    last = f(uT, bank[:, 0:TOK], ACT.Gelu_apprx_tanh)
                else:
                    if before is not None:
                        act.wait_ge(E["mixB_r"], before)
                    last = f(zs, bank[:, 0:TOK], ACT.Silu)
                last.then_inc(piece_ev, 1)

            for s in range(PIECES):
                piece_out(s, s + 1, None)
            act.wait_ge(dec["prep_v"], 4)
            f(pre[:, 1], pre[:, 5], ACT.Exp)
            f(pre[:, 2], pre[:, 7], ACT.Exp).then_inc(dec["prep_a"], 1)

            def head(h, fill):
                snap = (lambda v: v) if isinstance(h, int) else act.snap
                if not isinstance(h, int):
                    ac.base, ac.n = act.snap(h * A_CHAIN + n_before), 0
                start = ac.n
                h1 = snap(h + 1)
                step = [0]

                def pieces_out():
                    if fill:
                        for s in range(PIECES):
                            if PIECE_AT[s] == step[0]:
                                piece_out(s, snap(h * PIECES + (PIECES + s + 1)), h1)
                    step[0] += 1

                v = snap(h * 96)
                act.wait_ge(E["cs_T"], h1)
                act.wait_ge(E["cs_st"], v)
                f(csT[0:27, :, :], ps[0:27, 4, 0:3 * P].rearrange("r (s n) -> r s n", s=3)).then_inc(E["cs_cp"], 1)
                pieces_out()
                act.wait_ge(E["conv_r"], h1)
                f(qkvT[:, :, 0:PROMPT], acc[:, :, 0:PROMPT], ACT.Silu)
                for s in range(3):
                    last = f(qkvT[:, s, PROMPT:TOK].rearrange("p (b c) -> p b c", c=SEQ_LEN),
                             acc_s[:, s], ACT.Silu)
                last.then_inc(E["qkv_r"], 1)
                act.wait_ge(E["qkv_r"], h1)
                f(sq[:, :, :], qkvT[:, 0:2, :], ACT.Square).then_inc(E["sq_r"], 1)
                act.wait_ge(E["ln_d"], h1)
                for t, (_, n) in enumerate(TILES):
                    last = f(lnj[0:n, t, :], vd[0:n, t, :], ACT.Square, accum_out=lnr[0:n, t:t + 1])
                ac(last)
                act.wait_ge(E["ss_mm"], h1)
                rstd([(rn[:, 0, :], ps[:, 2, 0:TOK], P), (rn[:, 1, :], ps[:, 4, 0:TOK], P)], 1, E["rn_r"])
                ac.wait()
                rstd([(lnq[:, :], lnr[:, :], P)], P, E["ln_sq"])
                pieces_out()
                act.wait_ge(E["dd_r"], h1)
                f(eG, ps[:, 2, 0:TOK], ACT.Exp)
                f(Dm[:, :, :], dd[:, :, :], ACT.Exp, scale=-1.0)
                f(Ds[0:SAMPLE, :], dds[0:SAMPLE, :], ACT.Exp, scale=-1.0).then_inc(E["D_r"], 1)
                for t, (_, n) in enumerate(TILES):
                    kt, vt = ps[0:n, 5, t * P:(t + 1) * P], ps[0:n, 6, t * P:(t + 1) * P]
                    f(kbg[0:n, t, :], kt, scale=hs[0:n, t, 3:4])
                    f(kd[0:n, t, :], kt, scale=hs[0:n, t, 4:5])
                    last = f(vb[0:n, t, :], vt, scale=hs[0:n, t, 2:3])
                last.then_inc(E["tok_cp"], 1)
                pieces_out()
                act.wait_ge(E["AT_mm"], h1)
                f(QKT[:, :, :], ps[:, 6, 0:256].rearrange("p (t n) -> p t n", t=2))
                f(QKTs[0:SAMPLE, :], ps[0:SAMPLE, 6, 256:256 + SAMPLE]).then_inc(E["QKT_r"], 1)
                pieces_out()
                for lev in range(1, LEVELS):
                    v = snap(h * (LEVELS - 1) + lev)
                    act.wait_ge(lev_mm, v)
                    last = f(T1[:, :, :], ps[:, 5, 0:256].rearrange("p (t n) -> p t n", t=2))
                    if lev == 1:
                        last = f(T1s[0:SAMPLE, :], ps[0:SAMPLE, 5, 256:256 + SAMPLE])
                    last.then_inc(lev_cp, 1)
                    pieces_out()
                    if lev == 2:
                        act.wait_ge(E["W_T"], h1)
                        f(WT, ps[:, 2, 0:P]).then_inc(E["WT_r"], 1)
                    pieces_out()
                act.wait_ge(E["uw_mm"], h1)
                f(us[:, :, :], ps[:, 5, 0:256].rearrange("p (t n) -> p t n", t=2))
                f(uTs, ps[:, 5, PROMPT:TOK])
                f(WQ[:, :, 0:SEQ_LEN], ps[:, 6, PROMPT:TOK].rearrange("p (b c) -> p b c", c=SEQ_LEN))
                f(wT[:, 1, :], ps[:, 6, P:2 * P]).then_inc(E["uw_cp"], 1)
                pieces_out()
                act.wait_ge(E["S1_mm"], h1)
                f(S1, ps[:, 7, 0:P]).then_inc(E["S1_r"], 1)
                pieces_out()
                act.wait_ge(E["vnTT"], h1)
                f(vns[0:SAMPLE, :], ps[0:SAMPLE, 5, 0:P]).then_inc(E["vns_r"], 1)
                pieces_out()
                act.wait_ge(E["o_mm"], h1)
                f(oS, ps[:, 4, 0:TOK]).then_inc(E["os_p"], 1)
                pieces_out()
                act.wait_ge(E["os_r"], h1)
                f(osq, oS, ACT.Square).then_inc(E["osq_r"], 1)
                act.wait_ge(E["oss_mm"], h1)
                rstd([(orn, ps[:, 3, 0:TOK], P)], P, E["or_r"])
                pieces_out()
                pieces_out()
                assert ac.n - start == A_CHAIN, ac.n - start

            act.wait_ge(dec["prep_v"], 5)
            n_before = ac.n
            with act.Fori(0, HEADS - 1) as h:
                head(h, True)
            ac.base, ac.n = None, n_before + (HEADS - 1) * A_CHAIN
            head(HEADS - 1, False)

            def sample_copies(sem_):
                for g in range(4):
                    last = f(smp[0:SAMPLE, g, :], ps[32 * g:32 * g + 32, 4, :])
                last.then_inc(sem_, 1)

            act.wait_ge(E["mixB_r"], HEADS)
            act.wait_ge(E["cs_st"], 6 * 16 * HEADS)
            act.wait_ge(E["va_st"], 16 * HEADS)
            act.wait_ge(E["s2_st"], 16 * HEADS)
            act.wait_ge(E["sn_st"], 16 * HEADS)
            act.dma_start(pin[:, 0:2, :], d["p_prompt"].rearrange("l b (t p) n -> p (l b t) n", p=P)).then_inc(F["p_in"], 16)
            act.dma_start(pin[0:SAMPLE, 2, :], d["p_sample"].rearrange("l b t n -> (l b t) n")).then_inc(F["p_in"], 16)
            for half in range(2):
                act.wait_ge(G["out_used"], 8 * (half + 1))
                if half:
                    act.wait_ge(G["smp_add"], 1)
                sample_copies(G["smp_cp"])

            act.wait_ge(G["out_add"], 2)
            act.wait_ge(G["smp_add"], 2)
            rms()
            tiles_out(1)
            act.wait_ge(R["route_in"], 1)
            f(rt[:, 1, :, 0:4], rt[:, 0, :, 0:4], ACT.Exp).then_inc(R["route_exp"], 1)
            act.wait_ge(R["route_in"], 2)
            f(rc[:, 5, :], rc[:, 4, :], ACT.Exp).then_inc(R["route_exp"], 1)

            act.wait_ge(R["rounds_r"], 1)
            rounds = act.value_load(rnd_i[0:1, 0:1], min_val=1, max_val=MAX_ROUNDS)

            def rows_out(j, bank):
                return f(xg[:, j * 512:(j + 1) * 512], ps[:, bank, :])

            with act.Fori(0, rounds) as r:
                q1 = act.snap(r * (PAIRS + 1) + 1)
                act.wait_ge(M["gathA"], q1)
                rows_out(1, 1).then_inc(M["xgA_a"], 1)
                act.wait_ge(M["gathB"], q1)
                rows_out(3, 7).then_inc(M["xgB_a"], 1)
                with act.Fori(0, PAIRS) as it:
                    n1 = act.snap(r * PAIRS + it + 1)
                    q2 = act.snap(r * (PAIRS + 1) + it + 2)
                    u0 = act.snap((r * PAIRS + it) * 24 + 8)
                    u1 = act.snap(u0 + 8)
                    u2 = act.snap(u0 + 16)
                    act.wait_ge(M["wpt_T"], n1)
                    f(wpT[:, :], ps[:, 2, 0:TOK]).then_inc(M["wpt_cp"], 1)
                    act.wait_ge(M["used"], u0)
                    f(gu[:, 0, :], ps[:, 4, :]).then_inc(M["s0"], 1)
                    act.wait_ge(M["gT0"], n1)
                    act.wait_ge(M["h0"], act.snap(n1 - 1))
                    f(sg[:, 0], ps[:, 2, :].rearrange("p (i s) -> p i s", i=4)[:, :, 0:CAP], ACT.Silu).then_inc(M["silu0"], 1)
                    act.wait_ge(M["used"], u1)
                    f(gu[:, 1, :], ps[:, 5, :]).then_inc(M["s1"], 1)
                    act.wait_ge(M["gathA"], q2)
                    rows_out(1, 1).then_inc(M["xgA_a"], 1)
                    act.wait_ge(M["gT1"], n1)
                    f(sg[:, 1], ps[:, 3, :].rearrange("p (i s) -> p i s", i=4)[:, :, 0:CAP], ACT.Silu).then_inc(M["silu1"], 1)
                    act.wait_ge(M["gathB"], q2)
                    rows_out(3, 7).then_inc(M["xgB_a"], 1)
                    act.wait_ge(M["used"], u2)
                    f(yx[:, 512:1024], ps[:, 1, :])
                    f(yx[:, 1536:2048], ps[:, 3, :]).then_inc(M["y_a"], 1)

            act.wait_ge(M["moe_v"], 1)
            rms()
            tiles_out(2)
            act.wait_ge(F["pT_T"], 1)
            for k in range(2):
                last = f(pT[:, k, :], ps[:, k, 0:TOK])
            last.then_inc(F["pT_r"], 1)
            for half in range(2):
                act.wait_ge(F["gate_used"], 8 * (half + 1))
                if half:
                    act.wait_ge(F["pp_r"], 6)
                for q in range(4):
                    f(sig[:, q, :], ps[:, q, :]).then_inc(F["sig_r"], 1)
                sample_copies(F["sigs_r"])
                act.wait_ge(F["sig_r"], 4 * (half + 1))
                for q in range(4):
                    last = f(sig[:, q, :], sig[:, q, :], ACT.Sigmoid)
                last.then_inc(F["sg_r"], 1)
                act.wait_ge(F["ssum"], half + 1)
                f(smp[0:SAMPLE, 0:2, :], smp[0:SAMPLE, 0:2, :], ACT.Sigmoid).then_inc(F["ssg_r"], 1)
            act.wait_ge(F["x_done"], 1)
            act.dma_start(gfin[:, :], d["g_final"].rearrange("(a n) -> a n", a=1).to_broadcast([P, D_MODEL])).then_inc(F["gf_in"], 16)
            rms()

        @block.vector
        def _(v):
            ch = Chain(v, vec_chain)
            ts, tt, st, cp = v.tensor_scalar, v.tensor_tensor, v.scalar_tensor_tensor, v.tensor_copy

            def bc(ap, shape):
                return ap.to_broadcast(shape)

            def seq(*makers):
                for m in makers:
                    ch(m())
                    ch.wait()

            def normalised_rows(ph):
                v.wait_ge(norm["rstd"], ph + 1)
                for t, (_, n) in enumerate(TILES):
                    ts(hn[0:n, t, :], x[0:n, t, :], rs2[0:n, t:t + 1], None, ALU.mult).then_inc(norm["hnorm"], 1)

            def tiles_out(ph):
                for k in range(0, KT, 2):
                    v.wait_ge(norm["tile_T"], KT * ph + k + 1)
                    ts(hT[:, k, :], ps[:, k % 8, 0:TOK], gT[:, ph, k:k + 1], None, ALU.mult).then_inc(norm["tile_out_v"], 1)

            v.memset(eps[:, :], EPS)
            v.memset(lnr[:, :], 1.0)
            v.memset(ss[:, :], 1.0).then_inc(norm["ss_zero"], 1)
            v.memset(lnm[:, :], 0.0)
            v.memset(ab[:, :, :], 0.0)
            v.memset(pre[:, :, :, :], 0.0)
            ch(v.memset(raw[:, :, 0:PAD], 0.0))
            v.wait_ge(dec["prep_mm"], 1)
            cp(cw[:, :, :, :], ps[:, 7, 0:96].rearrange("p (w s h) -> p w s h", w=TAPS, s=3))
            cp(gT[:, :, :], ps[:, 7, 96:144].rearrange("p (a k) -> p a k", a=3)).then_inc(dec["prep_v"], 1)
            v.wait_ge(dec["prep_v"], 1)
            v.wait_ge(ld["ld_x"], 32)
            normalised_rows(0)
            tiles_out(0)
            v.wait_ge(ld["ld_small"], 16 * 4)
            v.wait_ge(dec["prep_mm"], 2)
            cp(ab[:, 0:2, :], ps[:, 2, 0:32].rearrange("p (t c) -> p t c", t=2))
            ch(cp(ab[0:SAMPLE, 2, :], ps[0:SAMPLE, 2, 32:48]))
            ch.wait()
            for t in range(3):
                last = tt(pre[:, 1, t, :], ab[:, t, 0:HEADS], dtb[:, :], ALU.add)
            ch(last)
            ch.wait()
            st(out=pre[:, 2], in0=pre[:, 1], scalar=-1.0, in1=pre[:, 1], op0=ALU.mult, op1=ALU.max).then_inc(dec["prep_v"], 1)
            v.wait_ge(dec["prep_a"], 2)
            ch(ts(pre[:, 4], pre[:, 4], 1.0, None, ALU.add))
            ch(st(out=pre[:, 6], in0=pre[:, 1], scalar=0.0, in1=pre[:, 7], op0=ALU.max, op1=ALU.add))
            ch.wait()
            ch(v.reciprocal(pre[:, 3], pre[:, 4]))
            for t in range(3):
                last = st(out=pre[:, 0, t, :], in0=pre[:, 6, t, :], scalar=-1.0, in1=ngexp[:, :], op0=ALU.mult, op1=ALU.mult)
            last.then_inc(dec["prep_v"], 1)
            v.wait_ge(dec["prep_v"], 3)
            v.wait_ge(dec["prep_mm"], 3)
            cp(pre[:, 5, 0:2, :], ps[:, 3, 0:16].rearrange("p (t c) -> p t c", t=2))
            cp(pre[0:SAMPLE, 5, 2, :], ps[0:SAMPLE, 3, 16:24])
            cp(pre[:, 6, 0:2, :], ps[:, 3, 24:40].rearrange("p (t c) -> p t c", t=2))
            ch(cp(pre[0:SAMPLE, 6, 2, :], ps[0:SAMPLE, 3, 40:48]))
            ch.wait()
            tt(pre[:, 7, 0:2], pre[:, 6, 0:2], pre[:, 5, 0:2], ALU.subtract)
            v.memset(pre[:, 7, 2], 0.0)
            ch(v.memset(zero[:, :], 0.0))
            ch.wait()
            tt(pre[0:SAMPLE, 7, 2], pre[0:SAMPLE, 6, 2], pre[0:SAMPLE, 5, 2], ALU.subtract).then_inc(dec["prep_v"], 1)
            v.wait_ge(dec["prep_a"], 3)
            ch(tt(pre[:, 4], pre[:, 3], pre[:, 1], ALU.mult))
            ch.wait()
            for kind, src in enumerate((0, 5, 3, 4, 2)):
                last = cp(sc[:, :, :, kind].rearrange("p h t -> p t h"), pre[:, src])
            last.then_inc(dec["prep_v"], 1)
            v.wait_ge(dec["prep_v"], 5)
            n_before = ch.n

            def head(h, loop):
                snap = v.snap if loop else (lambda a: a)
                if loop:
                    ch.base, ch.n = v.snap(h * V_CHAIN + n_before), 0
                start = ch.n
                h1, h0 = snap(h + 1), snap(h + 0)
                cp(hs[:, :, :], sc[:, bass.ds(h, 1), :, :].rearrange("p a t k -> p (a t) k"))
                ch(cp(hcw[:, :, :], cw[:, :, :, bass.ds(h, 1)].rearrange("p w s a -> p w (s a)")))
                ch.wait()
                for t, (_, n) in enumerate(TILES):
                    ts(gcol[0:n, t, :], C("ones", n), hs[0:n, t, 0:1], None, ALU.mult)
                v.wait_ge(E["st_T"], h1)
                cp(raw_s[:, :, :, 0:PAD],
                   ps[:, 2, 0:72].rearrange("p (s b c) -> p s b c", s=3, c=PAD)).then_inc(E["st_in"], 1)
                v.wait_ge(piece_ev, snap(h * PIECES + (V + 1)))
                v.wait_ge(E["st_in"], h1)
                cp(cs[:, :, 0:PAD], raw[:, :, PROMPT:PROMPT + PAD])
                cp(cs[:, :, PAD:].rearrange("p s (b c) -> p s b c", c=PAD), raw_s[:, :, :, SEQ_LEN:]).then_inc(E["cs_r"], 1)
                for s in range(3):
                    ch(ts(acc[:, s, 0:RAW - PAD], raw[:, s, 0:RAW - PAD], hcw[:, 0, s:s + 1], None, ALU.mult))
                for j in range(1, TAPS):
                    ch.wait()
                    for s in range(3):
                        last = st(out=acc[:, s, 0:RAW - PAD], in0=raw[:, s, j:j + RAW - PAD], scalar=hcw[:, j, s:s + 1],
                                  in1=acc[:, s, 0:RAW - PAD], op0=ALU.mult, op1=ALU.add)
                        if s == 2 and j == TAPS - 1:
                            last.then_inc(E["conv_r"], 1)
                        else:
                            ch(last)
                v.wait_ge(E["vaT_T"], h1)
                v.tensor_reduce(lnm[:, 0:2], ps[:, 3, 0:256].rearrange("p (t n) -> p t n", t=2), AX, ALU.add)
                ch(v.tensor_reduce(lnm[0:SAMPLE, 2:3], ps[0:SAMPLE, 3, 256:384], AX, ALU.add))
                ch.wait()
                ch(ts(lns[:, :], lnm[:, :], -1.0 / P, None, ALU.mult))
                ch.wait()
                for t, (_, n) in enumerate(TILES):
                    last = ts(vd[0:n, t, :], ps[0:n, 3, t * P:(t + 1) * P], lns[0:n, t:t + 1], None, ALU.add)
                last.then_inc(E["ln_d"], 1)
                v.wait_ge(E["rn_r"], h1)
                st(out=qk[:, 0, :], in0=qkvT[:, 0, :], scalar=float(P) ** -0.5, in1=rn[:, 0, :], op0=ALU.mult, op1=ALU.mult)
                tt(qk[:, 1, :], qkvT[:, 1, :], rn[:, 1, :], ALU.mult).then_inc(E["qk_r"], 1)
                v.wait_ge(E["tok_mm"], h1)
                for t in range(2):
                    ts(dd[:, t, :], ps[:, 2, t * P:(t + 1) * P], hs[:, t, 1:2], 0.0, ALU.subtract, ALU.max)
                ts(dds[0:SAMPLE, :], ps[0:SAMPLE, 2, PROMPT:TOK], hs[0:SAMPLE, 2, 1:2], 0.0, ALU.subtract,
                   ALU.max).then_inc(E["dd_r"], 1)
                v.wait_ge(E["qk_r"], h1)
                v.wait_ge(E["D_r"], h1)
                tt(qg, qk[:, 0, :], eG, ALU.mult)
                for t in range(2):
                    tt(DS[:, t, :], Dm[:, t, :], C("strict"), ALU.mult)
                    tt(DC[:, t, :], Dm[:, t, :], C("causal"), ALU.mult)
                tt(DSs[0:SAMPLE, :], Ds[0:SAMPLE, :], C("bstrict", SAMPLE), ALU.mult)
                ch(tt(DCs[0:SAMPLE, :], Ds[0:SAMPLE, :], C("bcausal", SAMPLE), ALU.mult))
                ch.wait()
                for t in range(2):
                    st(out=Am[:, t, :], in0=ps[:, 7, t * P:(t + 1) * P], scalar=hs[:, t, 2:3], in1=DS[:, t, :],
                       op0=ALU.mult, op1=ALU.mult)
                tt(QKm[:, :, :], ps[:, 7, 256:512].rearrange("p (t n) -> p t n", t=2), DC[:, :, :], ALU.mult)
                st(out=Ams[0:SAMPLE, :], in0=ps[0:SAMPLE, 4, 0:SAMPLE], scalar=hs[0:SAMPLE, 2, 2:3], in1=DSs[0:SAMPLE, :],
                   op0=ALU.mult, op1=ALU.mult)
                tt(QKms[0:SAMPLE, :], ps[0:SAMPLE, 4, SAMPLE:2 * SAMPLE], DCs[0:SAMPLE, :], ALU.mult).then_inc(E["A_r"], 1)
                v.wait_ge(E["A_r"], h1)
                for t in range(2):
                    st(out=X[:, t, :], in0=Am[:, t, :], scalar=-1.0, in1=C("low0"), op0=ALU.mult, op1=ALU.mult)
                ch(st(out=Xs[0:SAMPLE, :], in0=Ams[0:SAMPLE, :], scalar=-1.0, in1=C("low0", SAMPLE, SAMPLE), op0=ALU.mult,
                      op1=ALU.mult))
                v.wait_ge(E["AT_mm"], h1)
                for lev in range(LEVELS):
                    for t in range(2):
                        last = tt(NT[:, lev, t, :], ps[:, 5, t * P:(t + 1) * P], C(f"mt{lev}"), ALU.mult)
                for lev in range(2):
                    last = tt(NTs[0:SAMPLE, lev, :], ps[0:SAMPLE, 5, 256:256 + SAMPLE], C(f"mt{lev}", SAMPLE, SAMPLE), ALU.mult)
                ch(last)
                ch.wait()
                for t in range(2):
                    tt(X[:, t, :], X[:, t, :], C("ident"), ALU.add)
                    st(out=XT[:, t, :], in0=NT[:, 0, t, :], scalar=-1.0, in1=C("ident"), op0=ALU.mult, op1=ALU.add)
                tt(Xs[0:SAMPLE, :], Xs[0:SAMPLE, :], C("ident", SAMPLE, SAMPLE), ALU.add)
                st(out=XTs[0:SAMPLE, :], in0=NTs[0:SAMPLE, 0, :], scalar=-1.0, in1=C("ident", SAMPLE, SAMPLE), op0=ALU.mult,
                   op1=ALU.add).then_inc(E["NT_r"], 1)
                v.wait_ge(E["NT_r"], h1)
                for lev in range(1, LEVELS):
                    if lev > 1:
                        v.wait_ge(lev_new, snap(h * (LEVELS - 1) + lev - 1))
                    lv = snap(h * (LEVELS - 1) + lev)
                    v.wait_ge(lev_x, lv)
                    two = lambda b: ps[:, b, 0:256].rearrange("p (t n) -> p t n", t=2)
                    if lev < LEVELS - 1:
                        tt(X[:, :, :], X[:, :, :], two(6), ALU.subtract)
                    if lev == 1:
                        tt(XTs[0:SAMPLE, :], XTs[0:SAMPLE, :], ps[0:SAMPLE, 7, 256:256 + SAMPLE], ALU.subtract)
                    tt(XT[:, :, :], XT[:, :, :], two(7), ALU.subtract).then_inc(lev_new, 1)
                    if lev == 1:
                        w48 = snap(h * 48 + 48)
                        v.wait_ge(E["w_ld"], w48)
                        tt(Wm, Wh, C("causal"), ALU.mult).then_inc(E["W_r"], 1)
                        v.wait_ge(E["ln_sq"], h1)
                        v.wait_ge(E["va_st"], snap(h * 16))
                        for t, (_, n) in enumerate(TILES):
                            last = st(out=vn[0:n, t, :], in0=vd[0:n, t, :], scalar=lnq[0:n, t:t + 1], in1=gB[0:n, :],
                                      op0=ALU.mult, op1=ALU.mult)
                        last.then_inc(E["vn_r"], 1)
                    if lev == 3:
                        v.wait_ge(E["Wrep"], h1)
                        for b in range(SEQS):
                            last = tt(WTs[0:SAMPLE, b * 4:b * 4 + 4], ps[0:SAMPLE, 3, 0:SEQ_LEN],
                                      C("ball", SAMPLE)[:, b * 4:b * 4 + 4], ALU.mult)
                        last.then_inc(E["WTs_r"], 1)
                    if lev == 5:
                        v.wait_ge(E["mixA_mm"], h1)
                        for t in range(2):
                            tt(mA[:, t * P:(t + 1) * P], ps[:, 4, t * P:(t + 1) * P], bB, ALU.add)
                        for b in range(SEQS):
                            at = PROMPT + b * SEQ_LEN
                            last = tt(mA[:, at:at + SEQ_LEN], ps[:, 4, at:at + SEQ_LEN], bB[:, 0:SEQ_LEN], ALU.add)
                        ch(last)
                        ch.wait()
                        tt(mixT[:, bass.ds(h, 1), :].rearrange("p a n -> p (a n)"), mA, uT, ALU.mult).then_inc(E["mixA_r"], 1)
                cp(WQ[:, :, SEQ_LEN:], qg[:, PROMPT:TOK].rearrange("p (b c) -> p b c", c=SEQ_LEN)).then_inc(E["WQ_r"], 1)
                v.wait_ge(E["SQ_mm"], h1)
                SQ = ps[:, 2, 0:64].rearrange("p (b c) -> p b c", c=8)
                sq4 = lambda a: a.rearrange("p (b c) -> p b c", c=SEQ_LEN)
                tt(sq4(vnTs), sq4(uTs), SQ[:, :, 0:SEQ_LEN], ALU.subtract).then_inc(E["vnT_r"], 1)
                v.wait_ge(E["wS_mm"], h1)
                tt(vn1, us[:, 1, :], ps[:, 3, 0:P], ALU.subtract).then_inc(E["vn1_r"], 1)
                v.wait_ge(E["vns_r"], h1)
                for b in range(SEQS):
                    last = ts(Vm[0:SAMPLE, b, :], vns[0:SAMPLE, :], C("seq", SAMPLE)[:, b:b + 1], None, ALU.mult)
                last.then_inc(E["Vm_r"], 1)
                v.wait_ge(E["os_p"], h1)
                os4 = sq4(oS[:, PROMPT:TOK])
                tt(os4, os4, SQ[:, :, SEQ_LEN:], ALU.add).then_inc(E["os_r"], 1)
                v.wait_ge(E["s2_st"], snap(h * 16))
                st(out=S2, in0=S1, scalar=eG[:, 2 * P - 1:2 * P], in1=ps[:, 7, P:2 * P], op0=ALU.mult,
                   op1=ALU.add).then_inc(E["S2_r"], 1)
                v.wait_ge(E["dS_mm"], h1)
                v.wait_ge(E["sn_st"], snap(h * 16))
                for b in range(SEQS):
                    at = PROMPT + b * SEQ_LEN + SEQ_LEN - 1
                    last = st(out=Snew[:, b, :], in0=Sold[:, b, :], scalar=eG[:, at:at + 1],
                              in1=ps[:, 5 + b // 4, (b % 4) * P:(b % 4 + 1) * P], op0=ALU.mult, op1=ALU.add)
                last.then_inc(E["Sn_r"], 1)
                v.wait_ge(piece_ev, snap((h + 1) * PIECES))
                v.wait_ge(E["osq_r"], h1)
                ch(st(out=ot, in0=oS, scalar=goutT[:, 0:1], in1=zs, op0=ALU.mult, op1=ALU.mult))
                ch.wait()
                v.wait_ge(E["or_r"], h1)
                tt(mixT[:, bass.ds(h + HEADS, 1), :].rearrange("p a n -> p (a n)"), ot, orn, ALU.mult).then_inc(E["mixB_r"], 1)
                v.wait_ge(E["mixB_r"], h1)
                assert ch.n - start == V_CHAIN, ch.n - start

            with v.Fori(0, HEADS - 1) as h:
                head(h, True)
            ch.base, ch.n = None, n_before + (HEADS - 1) * V_CHAIN
            head(HEADS - 1, False)

            for half in range(2):
                c0 = half * 1024
                v.wait_ge(G["out_used"], 8 * (half + 1))
                for t in range(2):
                    for n in range(2):
                        xs = x[:, t, c0 + n * 512:c0 + (n + 1) * 512]
                        last = tt(xs, xs, ps[:, 2 * t + n, :], ALU.add)
                last.then_inc(G["out_add"], 1)
                v.wait_ge(G["smp_cp"], half + 1)
                xs = x[0:SAMPLE, 2, c0:c0 + 1024].rearrange("p (n c) -> p n c", n=2)
                ch(tt(xs, xs, smp[0:SAMPLE, 0:2, :], ALU.add))
                ch.wait()
                tt(xs, xs, smp[0:SAMPLE, 2:4, :], ALU.add).then_inc(G["smp_add"], 1)

            v.wait_ge(G["out_add"], 2)
            v.wait_ge(G["smp_add"], 2)
            normalised_rows(1)
            tiles_out(1)
            v.memset(lg[:, :, :], 0.0)
            v.memset(rankm[:, :, :], FAR)
            ch(v.memset(wt[:, :, :], 0.0))
            ch.wait()
            v.wait_ge(ld["ld_route"], 16 * 5)
            v.wait_ge(R["route_mm"], 1)
            for t, (_, n) in enumerate(TILES):
                last = tt(lg[0:n, t, :], ps[0:n, 0, t * 36:(t + 1) * 36], rbias[0:n, :], ALU.add)
            ch(last)
            ch.wait()
            gl, el = lg[:, :, 0:GROUPS], lg[:, :, GROUPS:]
            c3 = lambda a, n: a.unsqueeze(2).to_broadcast([P, 3, n])

            def first_max(val, n, mx, one):
                t = rt[:, 2, :, 0:n]
                seq(lambda: v.tensor_reduce(mx, val, AX, ALU.max),
                    lambda: tt(t, val, c3(mx, n), ALU.is_equal))
                for q in range(3):
                    last = st(out=rt[:, 3, q, 0:n], in0=rt[:, 2, q, 0:n], scalar=-99.0, in1=C("iota99")[:, 0:n],
                              op0=ALU.mult, op1=ALU.add)
                ch(last)
                ch.wait()
                seq(lambda: v.tensor_reduce(rc[:, 1, :], rt[:, 3, :, 0:n], AX, ALU.min),
                    lambda: tt(one, rt[:, 3, :, 0:n], c3(rc[:, 1, :], n), ALU.is_equal))

            first_max(gl, GROUPS, rc[:, 0, :], rt[:, 4, :, 0:GROUPS])
            tt(rt[:, 0, :, 0:4], gl, c3(rc[:, 0, :], GROUPS), ALU.subtract).then_inc(R["route_in"], 1)
            ch(ts(rt[:, 4, :, 8:12], rt[:, 4, :, 0:GROUPS], 1e30, -1e30, ALU.mult, ALU.add))
            ch.wait()
            for g in range(GROUPS):
                sl = slice(g * PER_GROUP, (g + 1) * PER_GROUP)
                last = tt(rt[:, 5, :, sl], el[:, :, sl], rt[:, 4, :, g:g + 1].to_broadcast([P, 3, PER_GROUP]), ALU.mult)
            ch(last)
            ch.wait()
            for g in range(GROUPS):
                sl = slice(g * PER_GROUP, (g + 1) * PER_GROUP)
                last = tt(rt[:, 6, :, sl], rt[:, 5, :, sl], rt[:, 4, :, 8 + g:9 + g].to_broadcast([P, 3, PER_GROUP]), ALU.add)
            ch(last)
            ch.wait()
            first_max(rt[:, 6], EXPERTS, rc[:, 3, :], rt[:, 7])
            seq(lambda: st(out=rt[:, 5], in0=rt[:, 7], scalar=-3e30, in1=rt[:, 6], op0=ALU.mult, op1=ALU.add))
            first_max(rt[:, 5], EXPERTS, rc[:, 6, :], rt[:, 8])
            tt(rc[:, 4, :], rc[:, 6, :], rc[:, 3, :], ALU.subtract).then_inc(R["route_in"], 1)
            tt(asg[:, :, :], rt[:, 7], rt[:, 8], ALU.add).then_inc(R["asg_r"], 1)
            v.wait_ge(R["route_exp"], 1)
            seq(lambda: v.tensor_reduce(rc[:, 7, :], rt[:, 1, :, 0:4], AX, ALU.add),
                lambda: v.reciprocal(rc[:, 2, :], rc[:, 7, :]))
            v.wait_ge(R["route_exp"], 2)
            seq(lambda: ts(rc[:, 8, :], rc[:, 5, :], 1.0, None, ALU.add),
                lambda: v.reciprocal(rc[:, 9, :], rc[:, 8, :]),
                lambda: tt(rc[:, 10, :], rc[:, 9, :], rc[:, 2, :], ALU.mult),
                lambda: tt(rc[:, 11, :], rc[:, 10, :], rc[:, 5, :], ALU.mult))
            tt(rt[:, 7], rt[:, 7], c3(rc[:, 10, :], EXPERTS), ALU.mult)
            seq(lambda: tt(rt[:, 8], rt[:, 8], c3(rc[:, 11, :], EXPERTS), ALU.mult),
                lambda: tt(wt[:, :, 0:EXPERTS], rt[:, 7], rt[:, 8], ALU.add))
            v.wait_ge(R["asg_r"], 1)
            v.wait_ge(R["route_mm"], 2)
            ch(v.tensor_reduce(cnt[:, :], ps[:, 1, 96:128], AX, ALU.max))
            ch(ts(rt[:, 3], asg[:, :, :], -FAR, FAR, ALU.mult, ALU.add))
            ch.wait()
            for t, (_, n) in enumerate(TILES):
                last = tt(rankm[0:n, t, 0:EXPERTS], rt[0:n, 3, t, :], ps[0:n, 1, t * 32:(t + 1) * 32], ALU.add)
            ch(last)
            for q in range(1, MAX_ROUNDS):
                last = ts(rnd[:, q:q + 1], cnt[:, :], float(CAP * q), None, ALU.is_gt)
            ch(last)
            ch(v.memset(rnd[:, 0:1], 1.0))
            ch.wait()
            seq(lambda: v.tensor_reduce(cnt[:, :], rnd[:, :], AX, ALU.add))
            cp(rnd_i[:, :], cnt[:, :]).then_inc(R["rounds_r"], 1)
            v.wait_ge(R["rounds_r"], 1)

            rounds = v.value_load(rnd_i[0:1, 0:1], min_val=1, max_val=MAX_ROUNDS)

            def one_hots(e0):
                for t, (_, n) in enumerate(TILES):
                    for ex in range(2):
                        last = ts(Pm[0:n, t, ex * CAP:(ex + 1) * CAP], C("iota", n), rankm[0:n, t, bass.ds(e0 + ex, 1)],
                                  None, ALU.is_equal)
                last.then_inc(M["P_r"], 1)

            def weighted(e0):
                for t, (_, n) in enumerate(TILES):
                    for ex in range(2):
                        last = ts(WP[0:n, t, ex * CAP:(ex + 1) * CAP], C("iota", n), rankm[0:n, t, bass.ds(e0 + ex, 1)],
                                  wt[0:n, t, bass.ds(e0 + ex, 1)], ALU.is_equal, ALU.mult)
                last.then_inc(M["WP_r"], 1)

            def rows_out(j, bank):
                return cp(xg[:, j * 512:(j + 1) * 512], ps[:, bank, :])

            def xT_out():
                for j in range(4):
                    for i in range(4):
                        k = 4 * j + i
                        last = ts(xT[:, k, :], ps[:, 4 + j, i * P:(i + 1) * P], gJ[:, k:k + 1], None, ALU.mult)
                last.then_inc(M["xT_r"], 1)

            with v.Fori(0, rounds) as r:
                q1 = v.snap(r * (PAIRS + 1) + 1)
                n0 = v.snap(r * PAIRS)
                one_hots(0)
                weighted(0)
                v.wait_ge(M["gathA"], q1)
                rows_out(0, 0).then_inc(M["xgA_v"], 1)
                v.wait_ge(M["gathB"], q1)
                rows_out(2, 6).then_inc(M["xgB_v"], 1)
                v.wait_ge(M["xT_T"], q1)
                xT_out()
                with v.Fori(0, PAIRS) as it:
                    n1 = v.snap(r * PAIRS + it + 1)
                    n0 = v.snap(n1 - 1)
                    q2 = v.snap(r * (PAIRS + 1) + it + 2)
                    u2 = v.snap((r * PAIRS + it) * 24 + 24)
                    e2 = v.snap(it * 2 + 2)
                    one_hots(e2)
                    v.wait_ge(M["wpt_T"], n1)
                    weighted(e2)
                    v.wait_ge(M["silu0"], n1)
                    tt(hx[:, 0], sg[:, 0], ps[:, 2, :].rearrange("p (i s) -> p i s", i=4)[:, :, CAP:], ALU.mult).then_inc(M["h0"], 1)
                    v.wait_ge(M["gathA"], q2)
                    rows_out(0, 0).then_inc(M["xgA_v"], 1)
                    v.wait_ge(M["silu1"], n1)
                    tt(hx[:, 1], sg[:, 1], ps[:, 3, :].rearrange("p (i s) -> p i s", i=4)[:, :, CAP:], ALU.mult).then_inc(M["h1"], 1)
                    v.wait_ge(M["gathB"], q2)
                    rows_out(2, 6).then_inc(M["xgB_v"], 1)
                    v.wait_ge(M["used"], u2)
                    cp(yx[:, 0:512], ps[:, 0, :])
                    cp(yx[:, 1024:1536], ps[:, 2, :]).then_inc(M["y_v"], 1)
                    v.wait_ge(M["xT_T"], q2)
                    xT_out()
                    v.wait_ge(M["add2"], n0)
                    for t, (_, n) in enumerate(TILES):
                        v.wait_ge(M[f"c{t}"], n1)
                        for c in range(2):
                            xs = x[0:n, t, c * 1024:(c + 1) * 1024].rearrange("p (a b) -> p a b", a=2)
                            b0 = (t % 2) * 4 + 2 * c
                            last = tt(xs, xs, ps[0:n, b0:b0 + 2, :], ALU.add)
                        last.then_inc(M[f"add{t}"], 1)
                e_end = v.snap((r + 1) * (PAIRS + 1))
                v.wait_ge(M["P_r"], e_end)
                v.wait_ge(M["WP_r"], e_end)
                ts(rankm[:, :, :], rankm[:, :, :], -float(CAP), None, ALU.add).then_inc(M["rank_r"], 1)
                v.wait_ge(M["rank_r"], v.snap(r + 1))
                v.wait_ge(M["add2"], v.snap((r + 1) * PAIRS))
            v.memset(zero[:, :], 0.0).then_inc(M["moe_v"], 1)

            normalised_rows(2)
            tiles_out(2)
            for half in range(2):
                c0 = half * 1024
                v.wait_ge(F["sigs_r"], half + 1)
                tt(smp[0:SAMPLE, 0:2, :], smp[0:SAMPLE, 0:2, :], smp[0:SAMPLE, 2:4, :], ALU.add).then_inc(F["ssum"], 1)
                v.wait_ge(F["sg_r"], half + 1)
                for n in range(2):
                    for t in range(3):
                        m = TILES[t][1]
                        v.wait_ge(F["pp_mm"], half * 6 + n * 3 + t + 1)
                        if t == 2 and n == 0:
                            v.wait_ge(F["ssg_r"], half + 1)
                        gate = sig[:, 2 * t + n, :] if t < 2 else smp[0:SAMPLE, n, :]
                        tt(tmp[0:m, n * 3 + t, :], gate, ps[0:m, 5 + t, :], ALU.mult).then_inc(F["pp_r"], 1)
                v.wait_ge(F["pp_r"], 6 * (half + 1))
                for n in range(2):
                    for t in range(3):
                        m = TILES[t][1]
                        xs = x[0:m, t, c0 + n * 512:c0 + (n + 1) * 512]
                        last = tt(xs, xs, tmp[0:m, n * 3 + t, :], ALU.add)
                if half:
                    last.then_inc(F["x_done"], 1)
                    v.wait_ge(F["x_done"], 1)
                else:
                    ch(last)
                    ch.wait()
            v.wait_ge(norm["rstd"], 4)
            v.wait_ge(F["gf_in"], 16)
            for t, (_, n) in enumerate(TILES):
                st(out=x[0:n, t, :], in0=x[0:n, t, :], scalar=rs2[0:n, t:t + 1], in1=gfin[0:n, :], op0=ALU.mult,
                   op1=ALU.mult).then_inc(F["y_r"], 1)


_INS = ["x_prompt", "x_sample", "state_conv", "state_delta", "p_prompt", "p_sample", "w_in", "w_s", "b_s", "g_v", "g_mix",
        "conv_w", "a_log", "dt_bias", "g_out", "w_out", "g_ffn", "w_group", "b_group", "w_router", "b_router", "w_gate",
        "w_up", "w_down", "g_ple", "w_ple_gate", "w_ple", "g_final"]
_OUTS = [(1, PROMPT, D_MODEL), (SEQS, SEQ_LEN, D_MODEL), (1, 1, PAD, CONV_DIM), (1, 1, HEADS, P, P),
         (1, SEQS, PAD, CONV_DIM), (1, SEQS, HEADS, P, P), (1, SEQS, SEQ_LEN, WIDTH)]


def kernel(**inputs):
    import concourse.bacc as _bacc
    from concourse.bass_utils import run_bass_kernel_spmd as _run

    nc = _bacc.Bacc("TRN2", target_bir_lowering=False, num_devices=1)
    arrays, d = {}, {}
    for name in _INS:
        a = np.ascontiguousarray(inputs[name])
        arrays[f"in_{name}_dram"] = a
        d[name] = nc.dram_tensor(f"in_{name}_dram", a.shape, F32, kind="ExternalInput").ap()
    arrays["in_consts_dram"] = _constants()
    d["consts"] = nc.dram_tensor("in_consts_dram", (P, N_CONST), F32, kind="ExternalInput").ap()
    outs = [nc.dram_tensor(f"out_{i}_dram", shape, F32, kind="ExternalOutput").ap() for i, shape in enumerate(_OUTS)]
    trunk(nc, d, outs)
    r = _run(nc, [arrays], core_ids=[0])
    return tuple(r.results[0][f"out_{i}_dram"] for i in range(len(_OUTS)))
```

```python
from contextlib import ExitStack

import numpy as np

import concourse.bass as bass
from concourse import mybir

F32 = mybir.dt.float32
I32 = mybir.dt.int32
ALU = mybir.AluOpType
ACT = mybir.ActivationFunctionType
AX = mybir.AxisListType.X

P = 128
D_MODEL = 2048
KT = D_MODEL // P
PROMPT = 256
SEQS, SEQ_LEN = 8, 4
SAMPLE = SEQS * SEQ_LEN
TOK = PROMPT + SAMPLE
TILES = ((0, 128), (128, 128), (256, SAMPLE))
HEADS = 8
WIDTH = 1024
CONV_DIM = 3 * WIDTH
TAPS = 4
PAD = TAPS - 1
SROW = PAD + SEQ_LEN
RAW = PAD + PROMPT + SEQS * SROW
S_AT = PAD + PROMPT
LEVELS = 7
EXPERTS, GROUPS, PER_GROUP = 32, 4, 8
D_EXP = 512
CAP = 64
PAIRS = EXPERTS // 2
MAX_ROUNDS = -(-TOK // CAP)
PLE = 256
EPS = 1e-6
SLOTS, SLOT = 12, 2048
PIECES = 6
Q, K, V, VA, U, Z = range(PIECES)
MOE_SLOT = 16 % SLOTS
RING_BASE = [(HEADS if s < PIECES else 0) + (2 if s < MOE_SLOT else 1) for s in range(SLOTS)]
TAIL_SLOTS = SLOTS - 2
V_CHAIN, A_CHAIN = 19, 4
D_BANKS = (5, 6)
FAR = 1e6

CONSTS = {}


def _constants():
    a = np.arange(P)
    row, col = a[:, None], a[None, :]
    same = (row // SEQ_LEN) == (col // SEQ_LEN)
    parts = [("ident", row == col), ("triu", row <= col), ("before", row < col), ("ones", row >= 0 * col),
             ("causal", row >= col), ("strict", row > col),
             ("low0", (row % 2 == 1) & (col == row - 1))]
    for lev in range(LEVELS):
        b = 1 << lev
        parts.append((f"mt{lev}", (col // b % 2 == 1) & (row // b == col // b - 1)))
    parts += [("iota", np.broadcast_to(np.arange(CAP)[None, :], (P, CAP))),
              ("iota99", np.broadcast_to(99 + np.arange(EXPERTS)[None, :], (P, EXPERTS))),
              ("rep", row == a[None, :SAMPLE] % SEQ_LEN),
              ("seq", row // SEQ_LEN == np.arange(SEQS)[None, :]),
              ("btriu", (same & (row <= col))[:, :SAMPLE]), ("ball", same[:, :SAMPLE]),
              ("bcausal", (same & (row >= col))[:, :SAMPLE]), ("bstrict", (same & (row > col))[:, :SAMPLE])]
    at = 0
    for name, m in parts:
        CONSTS[name] = (at, m.shape[1])
        at += m.shape[1]
    return np.concatenate([m.astype(np.float32) for _, m in parts], axis=1)


N_CONST = _constants().shape[1]

AHEAD = 4
FILL = [15, 9, 12, 9] + [3, 2] * 5 + [2, 2] + [4, 4, 4, 4, 3]
FILL.append(PIECES * KT - sum(FILL))
LAST_FILL = [8, 3, 6, 5] + [1, 0] * 6 + [1, 1, 1, 1, 0, 0]


def piece_at(fill):
    return [next(n for n in range(len(fill)) if sum(fill[:n + 1]) >= KT * (i + 1)) for i in range(sum(fill) // KT)]


def tail_slot(c):
    return (MOE_SLOT + c % TAIL_SLOTS) % SLOTS


class Chain:

    def __init__(self, eng, sem):
        self.eng, self.sem, self.n, self.base = eng, sem, 0, None

    def __call__(self, ins):
        ins.then_inc(self.sem, 1)
        self.n += 1

    def wait(self):
        self.eng.wait_ge(self.sem, self.n if self.base is None else self.base + self.n)


def trunk(nc, d, o):
    ctx = ExitStack()
    with ctx:
        def sb(name, shape, dt=F32):
            return ctx.enter_context(nc.sbuf_tensor(name, shape, dt))

        def sem(name):
            return ctx.enter_context(nc.semaphore(name))

        def sems(*names):
            return {n: sem(n) for n in names}

        cst = sb("cst", [P, N_CONST])
        x = sb("x", [P, 3, D_MODEL])
        hb = sb("hb", [P, 3 * D_MODEL])
        hn = hb[:, :].rearrange("p (t d) -> p t d", t=3)
        hT = sb("hT", [P, KT, TOK])
        mixT = sb("mixT", [P, KT, TOK])
        ring = sb("ring", [P, SLOTS * SLOT])
        ps = ctx.enter_context(nc.psum_tensor("ps", [P, 8, 512], F32))

        def C(name, rows=P, cols=None):
            at, n = CONSTS[name]
            return cst[0:rows, at:at + (cols or n)]

        def slot(s):
            return ring[:, s * SLOT:(s + 1) * SLOT]

        class Carve:
            def __init__(self, *regions):
                self.regions = [[v, n, 0] for v, n in regions]

            def __call__(self, *shape):
                n = int(np.prod(shape))
                r = next(r for r in self.regions if r[2] + n <= r[1])
                v = r[0][:, r[2]:r[2] + n]
                r[2] += n
                if len(shape) == 2:
                    v = v.rearrange("p (a b) -> p a b", a=shape[0])
                elif len(shape) == 3:
                    v = v.rearrange("p (a b c) -> p a b c", a=shape[0], b=shape[1])
                return v

        grow = sb("grow", [3 * KT, P])
        gT = sb("gT", [P, 3, KT])
        gJ = sb("gJ", [P, KT])
        wab = sb("wab", [P, KT, 2 * HEADS])
        wr = sb("wr", [P, KT, GROUPS + EXPERTS])
        rbias = sb("rbias", [P, GROUPS + EXPERTS])
        goutT = sb("goutT", [P, 1])
        alog = sb("alog", [P, HEADS])
        dtb = sb("dtb", [P, HEADS])
        ss = sb("ss", [P, 3])
        rs2 = sb("rs2", [P, 3])
        ss_a = sb("ss_a", [P, 3])
        ln_b = sb("ln_b", [P, 3])
        cwr = sb("cwr", [TAPS * 3 * HEADS, P])
        cw = sb("cw", [P, TAPS, 3, HEADS])
        sc = sb("sc", [P, HEADS, 3, 5])
        hs = sb("hs", [P, 3, 5])
        hcw = sb("hcw", [P, TAPS, 3])
        ngexp = sb("ngexp", [P, HEADS])
        pre = sb("pre", [P, 8, 3, 8])
        ab = sb("ab", [P, 3, 16])

        more = sb("more", [P, 1152])
        w = Carve((ring[:, 6 * SLOT:12 * SLOT], 6 * SLOT), (hb[:, :], 3 * D_MODEL), (more[:, :], 1152))
        raw = w(3, RAW)
        raw_s = raw[:, :, S_AT:RAW].rearrange("p s (b c) -> p s b c", c=SROW)
        acc = w(3, RAW)
        acc_s = acc[:, :, S_AT:RAW].rearrange("p s (b c) -> p s b c", c=SROW)[:, :, :, 0:SEQ_LEN]
        qkvT = w(3, TOK)
        sq = w(2, TOK)
        rn = w(2, TOK)
        qk = w(2, TOK)
        gcol = w(3, P)
        dd = w(2, P)
        dds = w(SAMPLE)
        Dm = w(2, P)
        Ds = w(SAMPLE)
        DS = w(2, P)
        DSs = w(SAMPLE)
        eG = w(TOK)
        qg = w(TOK)
        Am = w(2, P)
        Ams = w(SAMPLE)
        QKm = w(2, P)
        QKms = w(SAMPLE)
        kbg = w(3, P)
        kd = w(3, P)
        vb = w(3, P)
        NT = w(LEVELS, 2, P)
        NTs = w(2, SAMPLE)
        QKT = w(2, P)
        QKTs = w(SAMPLE)
        X = w(2, P)
        XT = w(2, P)
        Xs = w(SAMPLE)
        XTs = w(SAMPLE)
        T1 = w(2, P)
        T1s = w(SAMPLE)
        us = w(2, P)
        wT = w(2, P)
        uTs = w(SAMPLE)
        WQ = w(SEQS, 2 * SEQ_LEN)
        S1 = w(P)
        S2 = w(P)
        vn1 = w(P)
        vnTs = w(SAMPLE)
        vns = w(P)
        Vm = w(SEQS, P)
        Sold = w(SEQS, P)
        Snew = w(SEQS, P)
        cs = w(3, PAD + SEQS * PAD)
        csT = w(3, P)
        stt = w(3, P)
        vaT = w(TOK)
        vd = w(3, P)
        vn = w(3, P)
        uT = w(TOK)
        zs = w(TOK)
        Wh = w(P)
        Wm = w(P)
        WT = w(P)
        WTs = w(SAMPLE)
        bB = w(P)
        gB = w(P)
        oS = w(TOK)
        osq, orn = rn[:, 0, :], rn[:, 1, :]
        ot = w(TOK)
        mA = ot
        DC = w(2, P)
        DCs = w(SAMPLE)
        lnj = Vm[:, 0:3, :]
        lnm, lns, lnr, lnq = (sb(n, [P, 3]) for n in ("lnm", "lns", "lnr", "lnq"))
        zero = sb("zero", [P, 1])
        eps = sb("eps", [P, 1])

        flat = mixT[:, :, :].rearrange("p k n -> p (k n)")
        wd = Carve((flat[:, D_MODEL:], KT * TOK - D_MODEL))
        lgT = more[0:GROUPS + EXPERTS, 3 * PLE:3 * PLE + TOK]
        lg = wd(3, GROUPS + EXPERTS)
        rt = wd(9, 3, EXPERTS)
        rc = wd(12, 3)
        asg = sb("asg", [P, 3, EXPERTS])
        rankm = sb("rankm", [P, 3, EXPERTS + 2])
        wt = sb("wt", [P, 3, EXPERTS + 2])
        cnt = sb("cnt", [P, 1])
        rnd = sb("rnd", [P, MAX_ROUNDS])
        rnd_i = sb("rnd_i", [P, 1], I32)

        we = Carve((flat, KT * TOK), (hT[:, :, :].rearrange("p k n -> p (k n)"), KT * TOK))
        xg = we(D_MODEL)
        yx = we(D_MODEL)
        hx = we(2, 4, CAP)
        xT = we(KT, P)
        gu = we(2, D_EXP)
        sg = we(2, 4, CAP)
        Pm = we(3, 2 * CAP)
        WP = we(3, 2 * CAP)
        wpT = sb("wpT", [P, TOK])

        wf = Carve((flat, KT * TOK))
        sig = wf(4, 512)
        pin = more[:, 0:3 * PLE].rearrange("p (t n) -> p t n", t=3)
        pT = wf(2, TOK)
        smp = hb[:, 0:4 * 512].rearrange("p (g n) -> p g n", g=4)
        tmp = hb[:, 4 * 512:10 * 512].rearrange("p (t n) -> p t n", t=3)
        squares = [ring[:, (6 + t) * SLOT:(7 + t) * SLOT] for t in range(3)]
        y = [ring[:, (9 + t) * SLOT:(10 + t) * SLOT] for t in range(3)]
        wp = ring[:, 2 * SLOT:4 * SLOT].rearrange("p (k n) -> p k n", k=2)
        gfin = ring[:, 4 * SLOT:5 * SLOT]

        ring_in = [sem(f"ring_in{s}") for s in range(SLOTS)]
        ld = sems("ld_const", "ld_x0", "ld_x1", "ld_x2", "ld_small", "ld_route", "ld_conv")
        vec_chain, act_chain = sem("vec_chain"), sem("act_chain")
        outs = sem("outs")
        norm = sems("ss_zero", "rstd", "hnorm", "tile_T", "tile_out_v", "tile_out_a")
        dec = sems("prep_mm", "prep_v", "prep_a")
        E = sems("st_ld", "w_ld", "s0_ld", "st_T", "st_in", "vaT_T", "conv_r", "cs_r", "cs_T",
                 "cs_cp", "cs_st", "va_st", "s2_st", "sn_st", "qkv_r", "sq_r", "ss_mm", "qk_r", "tok_mm", "dd_r", "D_r",
                 "tok_cp", "A_r", "AT_mm", "QKT_r", "NT_r", "W_r", "dS_mm", "W_T", "WT_r", "Wrep", "WTs_r", "ln_d",
                 "ln_sq", "vn_r", "mixA_mm", "mixA_r", "uw_mm", "uw_cp", "WQ_r", "S1_mm", "S1_r", "SQ_mm", "wS_mm",
                 "vn1_r", "vnT_r", "vnTT", "Vm_r", "vns_r", "o_mm", "S2_r", "Sn_r", "os_p", "os_r", "osq_r", "oss_mm", "rn_r", "or_r",
                 "mixB_r")
        lev_mm, lev_cp, lev_x, lev_new = sem("lev_mm"), sem("lev_cp"), sem("lev_x"), sem("lev_new")
        piece_mm, piece_ev = sem("piece_mm"), sem("piece_ev")
        G = sems("out_used", "out_add", "smp_cp", "smp_add")
        R = sems("lgT_mm", "lgT_r", "route_mm", "route_in", "route_exp", "asg_r", "rounds_r")
        M = sems("P_r", "WP_r", "wpt_T", "wpt_cp", "s0", "s1", "gT0", "gT1", "silu0", "silu1", "h0", "h1",
                 "gathA", "gathB", "rank_r", "xgA_v", "xgB_v", "xgA_a", "xgB_a", "y_v", "y_a", "xT_T", "xT_r",
                 "c0", "c1", "c2", "add0", "add1", "add2", "used", "moe_v")
        F = sems("p_in", "pT_T", "pT_r", "gate_used", "sigs_r", "ssum", "sg_r", "ssg_r", "pp_mm", "pp_r", "x_new", "xg_r",
                 "y_r", "y1_r", "gf_in", "wp_in")

        w_in = d["w_in"].rearrange("l (k p) n -> p (l k) n", p=P)
        conv_in = d["state_conv"].rearrange("l b r n -> (l b r) n")
        s_in = d["state_delta"].rearrange("l b h k v -> (l h) k b v")
        w_out = d["w_out"].rearrange("l (k p) n -> p (l k) n", p=P)
        w_pg = d["w_ple_gate"].rearrange("l (k p) n -> p (l k) n", p=P)
        w_gate = d["w_gate"].rearrange("l e (j p i) f -> (l e) j p (i f)", p=P, i=4)
        w_up = d["w_up"].rearrange("l e (j p i) f -> (l e) j p (i f)", p=P, i=4)
        w_down = d["w_down"].rearrange("l e (p i) n -> (l e) i p n", i=4)
        y_p, y_s, cv_p, sd_p, cv_s, sd_s, va_s = o
        y_p = y_p.rearrange("b (t p) n -> p (b t) n", p=P)
        y_s = y_s.rearrange("b l n -> (b l) n")
        cv_p = cv_p.rearrange("l b r n -> (l b r) n")
        cv_s = cv_s.rearrange("l b r n -> (l b r) n")
        sd_p = sd_p.rearrange("l b h k v -> (l b h) k v")
        sd_s = sd_s.rearrange("l b h k v -> (l h) k b v")
        va_s = va_s.rearrange("l b t n -> (l b t) n")
        piece_col = [2 * WIDTH, 3 * WIDTH, 4 * WIDTH, WIDTH, 0, 5 * WIDTH]

        block = ctx.enter_context(nc.Block())

        @block.sync
        def _(sp):
            for t in range(2):
                sp.dma_start(x[:, t, :], d["x_prompt"].rearrange("b (t p) n -> p (b t) n", p=P)[:, t, :]
                             ).then_inc(ld[f"ld_x{t}"], 16)
            sp.dma_start(x[0:SAMPLE, 2, :], d["x_sample"].rearrange("b l n -> (b l) n")).then_inc(ld["ld_x2"], 16)
            sp.dma_start(cst[:], d["consts"]).then_inc(ld["ld_const"], 16)

            def load_piece(s, col):
                sp.dma_start(slot(s).rearrange("p (k n) -> p k n", k=KT),
                             w_in[:, :, bass.ds(col, P)]).then_inc(ring_in[s], 16)

            def load_state(cols):
                for s in range(3):
                    sp.dma_start(stt[0:SEQS * PAD, s, :], conv_in[:, bass.ds(cols[s], P)]).then_inc(E["st_ld"], 16)

            def load_gate(h):
                sp.dma_start(Wh, d["w_s"].rearrange("l h t s -> (l h) t s")[bass.ds(h, 1)].rearrange("a t s -> (a t) s")
                             ).then_inc(E["w_ld"], 16)
                sp.dma_start(bB, d["b_s"][0:1, bass.ds(h, 1), :].rearrange("a b t -> (a b) t").to_broadcast([P, P])
                             ).then_inc(E["w_ld"], 16)
                sp.dma_start(gB, d["g_v"][0:1, bass.ds(h, 1), :].rearrange("a b t -> (a b) t").to_broadcast([P, P])
                             ).then_inc(E["w_ld"], 16)

            def load_delta(h):
                sp.dma_start(Sold, s_in[bass.ds(h, 1)].rearrange("a k b v -> (a k) b v")).then_inc(E["s0_ld"], 16)

            for s in range(PIECES):
                load_piece(s, piece_col[s])
            sp.wait_ge(norm["tile_T"], KT)
            load_state([s * WIDTH for s in range(3)])
            load_gate(0)
            load_delta(0)
            for s in range(AHEAD):
                sp.wait_ge(piece_mm, s + 1)
                load_piece(s, P + piece_col[s])

            def head(h, pieces, inputs):
                snap = (lambda v: v) if isinstance(h, int) else sp.snap
                c = [snap(h * P + s * WIDTH) for s in range(3)]
                c1 = [snap(h * P + (P + s * WIDTH)) for s in range(3)]
                h1 = snap(h + 1)

                def piece(i):
                    if i < pieces:
                        n, s = divmod(AHEAD + i, PIECES)
                        at = snap(h * PIECES + (AHEAD + i + 1))
                        col = snap(h * P + ((1 + n) * P + piece_col[s]))
                        sp.wait_ge(piece_mm, at)
                        load_piece(s, col)
                if inputs:
                    sp.wait_ge(E["st_in"], h1)
                    load_state(c1)
                sp.wait_ge(norm["tile_T"], KT)
                sp.wait_ge(E["cs_cp"], h1)
                for s in range(3):
                    sp.dma_start(cv_p[:, bass.ds(c[s], P)], csT[0:PAD, s, :]).then_inc(E["cs_st"], 16)
                    sp.dma_start(cv_s[:, bass.ds(c[s], P)], csT[PAD:PAD + SEQS * PAD, s, :]).then_inc(E["cs_st"], 16)
                piece(0)
                piece(1)
                sp.wait_ge(E["vn_r"], h1)
                sp.dma_start(va_s[:, bass.ds(c[0], P)], vn[0:SAMPLE, 2, :]).then_inc(E["va_st"], 16)
                piece(2)
                if inputs:
                    sp.wait_ge(E["mixA_r"], h1)
                    load_gate(h1)
                piece(3)
                sp.wait_ge(E["S2_r"], h1)
                sp.dma_start(sd_p[bass.ds(h, 1)].rearrange("a k v -> (a k) v"), S2).then_inc(E["s2_st"], 16)
                piece(4)
                sp.wait_ge(E["Sn_r"], h1)
                sp.dma_start(sd_s[bass.ds(h, 1)].rearrange("a k b v -> (a k) b v"), Snew).then_inc(E["sn_st"], 16)
                if inputs:
                    load_delta(h1)
                piece(5)

            with sp.Fori(0, HEADS - 2) as h:
                head(h, PIECES, True)
            head(HEADS - 2, PIECES - AHEAD, True)
            head(HEADS - 1, 0, False)

            for c in range(16):
                half, kk = divmod(c, 8)
                s = c % SLOTS
                if c < PIECES:
                    sp.wait_ge(piece_mm, (HEADS - 1) * PIECES + c + 1)
                elif c < SLOTS:
                    sp.wait_ge(E["mixB_r"], HEADS)
                    sp.wait_ge(E["cs_st"], 6 * 16 * HEADS)
                    sp.wait_ge(E["va_st"], 16 * HEADS)
                    sp.wait_ge(E["s2_st"], 16 * HEADS + 1)
                    sp.wait_ge(E["sn_st"], 16 * HEADS + 1)
                else:
                    sp.wait_ge(G["out_used"], c - SLOTS + 1)
                sp.dma_start(slot(s).rearrange("p (k n) -> p k n", k=2),
                             w_out[:, 2 * kk:2 * kk + 2, half * 1024:(half + 1) * 1024]).then_inc(ring_in[s], 16)

            def expert_of(c):
                return c // 8 if c < 16 else (c - 16) % 2

            def expert_chunk(c, e):
                r = c % 8 if c < 16 else (c - 16) // 2
                if c < 16:
                    src = (w_gate, w_up)[r % 2][bass.ds(e, 1), r // 2]
                else:
                    src = w_down[bass.ds(e, 1), r]
                s = (MOE_SLOT + c) % SLOTS
                sp.dma_start(slot(s), src.rearrange("a p n -> (a p) n")).then_inc(ring_in[s], 16)

            def gate_chunk(c):
                half, kk = divmod(c, 8)
                sp.dma_start(slot(tail_slot(c)).rearrange("p (k n) -> p k n", k=2),
                             w_pg[:, 2 * kk:2 * kk + 2, half * 1024:(half + 1) * 1024]).then_inc(ring_in[tail_slot(c)], 16)

            for c in range(SLOTS):
                sp.wait_ge(G["out_used"], c + 16 - SLOTS + 1)
                expert_chunk(c, expert_of(c))
            sp.wait_ge(R["rounds_r"], 1)
            rounds = sp.value_load(rnd_i[0:1, 0:1], min_val=1, max_val=MAX_ROUNDS)
            with sp.Fori(0, rounds) as r:
                with sp.Fori(0, PAIRS - 1) as it:
                    for c in range(24):
                        e = sp.snap(it * 2 + ((0 if c < 12 else 2) + expert_of((c + 12) % 24)))
                        first_down = 16 - 12
                        if c != first_down + 1:
                            k = sp.snap(r * (24 * PAIRS) + it * 24 + (c + (2 if c == first_down else 1)))
                            sp.wait_ge(M["used"], k)
                        expert_chunk((c + 12) % 24, e)
                for c in range(SLOTS):
                    k = sp.snap(r * (24 * PAIRS) + (24 * (PAIRS - 1) + c + 1))
                    sp.wait_ge(M["used"], k)
                    expert_chunk(c + 12, EXPERTS - 2 + expert_of(c + 12))
                k = [sp.snap(r * (24 * PAIRS) + (24 * (PAIRS - 1) + 12 + c + 1)) for c in range(SLOTS)]
                with sp.If(sp.snap(r + 1) < rounds):
                    for c in range(SLOTS):
                        sp.wait_ge(M["used"], k[c])
                        expert_chunk(c, expert_of(c))
                with sp.Else():
                    for c in range(TAIL_SLOTS):
                        sp.wait_ge(M["used"], k[c])
                        gate_chunk(c)
                    sp.wait_ge(M["used"], k[SLOTS - 1])
                    sp.dma_start(wp[:, :, :], d["w_ple"].rearrange("l (k p) n -> p (l k) n", p=P)).then_inc(F["wp_in"], 16)

            for c in range(TAIL_SLOTS, 16):
                sp.wait_ge(F["gate_used"], c - TAIL_SLOTS + 1)
                gate_chunk(c)
            sp.wait_ge(F["gate_used"], TAIL_SLOTS + 1)
            sp.dma_start(gfin[:, :], d["g_final"].rearrange("(a n) -> a n", a=1).to_broadcast([P, D_MODEL])).then_inc(F["gf_in"], 16)
            sp.wait_ge(F["y_r"], 1)
            sp.dma_start(y_p[:, 0, :], y[0]).then_inc(outs, 16)
            sp.wait_ge(F["y1_r"], 1)
            sp.dma_start(y_p[:, 1, :], y[1]).then_inc(outs, 16)
            sp.wait_ge(F["y_r"], 2)
            sp.dma_start(y_s, y[2][0:SAMPLE, :]).then_inc(outs, 16)
            sp.wait_ge(outs, 48)

        @block.tensor
        def _(pe):
            def mm(out, lhsT, rhs, start=True, stop=True):
                return pe.matmul(out, lhsT, rhs, start=start, stop=stop)

            def tr(out, in_, n):
                return pe.transpose(out, in_, C("ident", n, n))

            def tile_transposes(ph, src, ks, banks):
                for k in ks:
                    if k >= len(banks):
                        at = k - len(banks)
                        pe.wait_ge(norm["tile_out_a" if at % 2 else "tile_out_v"], 8 * ph + at // 2 + 1)
                    for t, (off, n) in enumerate(TILES):
                        last = tr(ps[:, banks[k % len(banks)], off:off + n], src[0:n, t, k * P:(k + 1) * P], n)
                    last.then_inc(norm["tile_T"], 1)

            def transposed(ph):
                pe.wait_ge(norm["tile_out_v"], 8 * (ph + 1))
                pe.wait_ge(norm["tile_out_a"], 8 * (ph + 1))

            pe.wait_ge(ld["ld_const"], 16)
            pe.wait_ge(ld["ld_conv"], 16 * 4)
            tr(ps[:, 7, 0:96], cwr[:, :], 96)
            tr(ps[:, 7, 96:96 + 3 * KT], grow[:, :], 3 * KT).then_inc(dec["prep_mm"], 1)
            pe.wait_ge(dec["prep_v"], 1)
            pe.wait_ge(norm["hnorm"], 3)
            tile_transposes(0, hn, range(KT), range(8))
            transposed(0)
            class Projection:

                def __init__(self, pieces):
                    self.at, self.pieces = 0, pieces

                def go(self, n):
                    for _ in range(min(n, KT * len(self.pieces) - self.at)):
                        i, k = divmod(self.at, KT)
                        self.at += 1
                        s, landed, emptied = self.pieces[i]
                        if k == 0:
                            pe.wait_ge(ring_in[s], landed)
                            if emptied is not None:
                                pe.wait_ge(piece_ev, emptied)
                        last = mm(ps[:, s % 2, 0:TOK], slot(s)[:, k * P:(k + 1) * P], hT[:, k, :], k == 0, k == KT - 1)
                        if k == KT - 1:
                            last.then_inc(piece_mm, 1)

            gemm = Projection([(s, 16, s - 1 if s >= 2 else None) for s in range(AHEAD)])
            gemm.go(2 * KT)
            pe.wait_ge(ld["ld_small"], 16 * 4)
            for t, (off, n) in enumerate(TILES):
                for k in range(KT):
                    last = mm(ps[0:n, 2, t * 16:(t + 1) * 16], hT[:, k, off:off + n], wab[:, k, :], k == 0, k == KT - 1)
            last.then_inc(dec["prep_mm"], 1)
            gemm.go((AHEAD - 2) * KT)

            pe.wait_ge(dec["prep_v"], 3)
            g = pre[:, 0]
            for t in range(2):
                mm(ps[:, 3, t * 8:t * 8 + 8], C("triu"), g[:, t, :])
                mm(ps[:, 3, 24 + t * 8:32 + t * 8], C("ones"), g[:, t, :])
            mm(ps[0:SAMPLE, 3, 16:24], C("btriu", SAMPLE), g[0:SAMPLE, 2, :])
            mm(ps[0:SAMPLE, 3, 40:48], C("ball", SAMPLE), g[0:SAMPLE, 2, :]).then_inc(dec["prep_mm"], 1)

            def head(h, fill):
                snap = (lambda v: v) if isinstance(h, int) else pe.snap
                h1 = snap(h + 1)
                gemm = Projection([((AHEAD + i) % PIECES, snap(h * 16 + 16 * (1 + (AHEAD + i) // PIECES)),
                                    snap(h * PIECES + (AHEAD + i - 1))) for i in range(PIECES if fill else PIECES - AHEAD)])
                step = [0]

                def next_head():
                    gemm.go((FILL if fill else LAST_FILL)[step[0]])
                    step[0] += 1

                pe.wait_ge(piece_ev, snap(h * PIECES + (VA + 1)))
                pe.wait_ge(E["st_ld"], snap((h + 1) * 48))
                for t, (off, n) in enumerate(TILES):
                    last = pe.transpose(ps[0:n, 3, t * P:(t + 1) * P], vaT[:, off:off + n], C("ident"))
                last.then_inc(E["vaT_T"], 1)
                for s in range(3):
                    last = tr(ps[:, 2, s * 24:(s + 1) * 24], stt[0:SEQS * PAD, s, :], SEQS * PAD)
                last.then_inc(E["st_T"], 1)
                pe.wait_ge(E["cs_r"], h1)
                for s in range(3):
                    last = tr(ps[0:27, 4, s * P:(s + 1) * P], cs[:, s, :], P)
                last.then_inc(E["cs_T"], 1)
                next_head()
                pe.wait_ge(E["sq_r"], h1)
                pe.wait_ge(E["st_in"], h1)
                pe.wait_ge(E["cs_cp"], h1)
                mm(ps[:, 2, 0:TOK], C("ones"), sq[:, 0, :])
                mm(ps[:, 4, 0:TOK], C("ones"), sq[:, 1, :]).then_inc(E["ss_mm"], 1)
                next_head()
                pe.wait_ge(E["qk_r"], h1)
                for t, (off, n) in enumerate(TILES):
                    pe.transpose(ps[0:n, 5, t * P:(t + 1) * P], qk[:, 1, off:off + n], C("ident"))
                    pe.transpose(ps[0:n, 6, t * P:(t + 1) * P], qkvT[:, 2, off:off + n], C("ident"))
                for t in range(2):
                    kt, qt = qk[:, 1, t * P:(t + 1) * P], qk[:, 0, t * P:(t + 1) * P]
                    mm(ps[:, 7, t * P:(t + 1) * P], kt, kt)
                    mm(ps[:, 7, 256 + t * P:256 + (t + 1) * P], qt, kt)
                    mm(ps[:, 2, t * P:(t + 1) * P], gcol[:, t, :], C("triu"))
                kt, qt = qk[:, 1, PROMPT:TOK], qk[:, 0, PROMPT:TOK]
                mm(ps[0:SAMPLE, 4, 0:SAMPLE], kt, kt)
                mm(ps[0:SAMPLE, 4, SAMPLE:2 * SAMPLE], qt, kt)
                mm(ps[:, 2, PROMPT:TOK], gcol[0:SAMPLE, 2, :], C("btriu", SAMPLE)).then_inc(E["tok_mm"], 1)
                next_head()
                pe.wait_ge(E["A_r"], h1)
                pe.wait_ge(E["tok_cp"], h1)
                pe.wait_ge(E["D_r"], h1)
                for t in range(2):
                    tr(ps[:, 5, t * P:(t + 1) * P], Am[:, t, :], P)
                    tr(ps[:, 6, t * P:(t + 1) * P], QKm[:, t, :], P)
                tr(ps[0:SAMPLE, 5, 256:256 + SAMPLE], Ams[0:SAMPLE, :], SAMPLE)
                tr(ps[0:SAMPLE, 6, 256:256 + SAMPLE], QKms[0:SAMPLE, :], SAMPLE).then_inc(E["AT_mm"], 1)
                next_head()
                for lev in range(1, LEVELS):
                    base = (LEVELS - 1)
                    v = snap(h * base + lev)
                    if lev == 1:
                        pe.wait_ge(E["NT_r"], h1)
                    else:
                        pe.wait_ge(lev_new, snap(h * base + lev - 1))
                    for t in range(2):
                        last = mm(ps[:, 5, t * P:(t + 1) * P], NT[:, lev, t, :], X[:, t, :])
                    if lev == 1:
                        last = mm(ps[0:SAMPLE, 5, 256:256 + SAMPLE], NTs[0:SAMPLE, 1, :], Xs[0:SAMPLE, :])
                    last.then_inc(lev_mm, 1)
                    next_head()
                    pe.wait_ge(lev_cp, v)
                    if lev == 1:
                        pe.wait_ge(E["QKT_r"], h1)
                    for t in range(2):
                        if lev < LEVELS - 1:
                            mm(ps[:, 6, t * P:(t + 1) * P], XT[:, t, :], T1[:, t, :])
                        last = mm(ps[:, 7, t * P:(t + 1) * P], T1[:, t, :], XT[:, t, :])
                    if lev == 1:
                        last = mm(ps[0:SAMPLE, 7, 256:256 + SAMPLE], T1s[0:SAMPLE, :], XTs[0:SAMPLE, :])
                    last.then_inc(lev_x, 1)
                    if lev == 2:
                        pe.wait_ge(E["W_r"], h1)
                        tr(ps[:, 2, 0:P], Wm, P).then_inc(E["W_T"], 1)
                    if lev == 3:
                        pe.wait_ge(E["WT_r"], h1)
                        mm(ps[0:SAMPLE, 3, 0:SEQ_LEN], C("rep"), WT[:, 0:SEQ_LEN]).then_inc(E["Wrep"], 1)
                    if lev == 5:
                        pe.wait_ge(E["WTs_r"], h1)
                        pe.wait_ge(E["vn_r"], h1)
                        for t in range(2):
                            mm(ps[:, 4, t * P:(t + 1) * P], vn[:, t, :], WT)
                        mm(ps[:, 4, PROMPT:TOK], vn[0:SAMPLE, 2, :], WTs[0:SAMPLE, :]).then_inc(E["mixA_mm"], 1)
                    next_head()
                pe.wait_ge(lev_new, snap((h + 1) * (LEVELS - 1)))
                for t in range(2):
                    mm(ps[:, 5, t * P:(t + 1) * P], XT[:, t, :], vb[:, t, :])
                    mm(ps[:, 6, t * P:(t + 1) * P], kbg[:, t, :], XT[:, t, :])
                mm(ps[:, 5, PROMPT:TOK], vb[0:SAMPLE, 2, :], XTs[0:SAMPLE, :])
                mm(ps[:, 6, PROMPT:TOK], kbg[0:SAMPLE, 2, :], XTs[0:SAMPLE, :]).then_inc(E["uw_mm"], 1)
                next_head()
                pe.wait_ge(E["uw_cp"], h1)
                pe.wait_ge(E["mixA_r"], h1)
                mm(ps[:, 7, 0:P], kd[:, 0, :], us[:, 0, :]).then_inc(E["S1_mm"], 1)
                mm(ps[:, 4, 0:P], us[:, 0, :], QKT[:, 0, :])
                pe.wait_ge(E["s0_ld"], snap((h + 1) * 16))
                pe.wait_ge(E["WQ_r"], h1)
                for b in range(SEQS):
                    last = mm(ps[:, 2, b * 8:(b + 1) * 8], Sold[:, b, :], WQ[:, b, :])
                last.then_inc(E["SQ_mm"], 1)
                next_head()
                pe.wait_ge(E["S1_r"], h1)
                mm(ps[:, 3, 0:P], wT[:, 1, :], S1).then_inc(E["wS_mm"], 1)
                pe.wait_ge(E["vnT_r"], h1)
                pe.transpose(ps[0:SAMPLE, 5, 0:P], vnTs, C("ident")).then_inc(E["vnTT"], 1)
                next_head()
                pe.wait_ge(E["vn1_r"], h1)
                mm(ps[:, 4, P:2 * P], S1, qg[:, P:2 * P], True, False)
                mm(ps[:, 4, P:2 * P], vn1, QKT[:, 1, :], False, True)
                mm(ps[:, 7, P:2 * P], kd[:, 1, :], vn1)
                pe.wait_ge(E["vns_r"], h1)
                mm(ps[:, 4, PROMPT:TOK], vns[0:SAMPLE, :], QKTs[0:SAMPLE, :]).then_inc(E["o_mm"], 1)
                next_head()
                pe.wait_ge(E["Vm_r"], h1)
                for q in range(2):
                    last = mm(ps[:, 5 + q, :], kd[0:SAMPLE, 2, :], Vm[0:SAMPLE, 4 * q:4 * q + 4, :])
                last.then_inc(E["dS_mm"], 1)
                pe.wait_ge(E["osq_r"], h1)
                mm(ps[:, 3, 0:TOK], C("ones"), osq).then_inc(E["oss_mm"], 1)
                next_head()
                next_head()
                pe.wait_ge(E["or_r"], h1)
                if fill:
                    pe.wait_ge(E["Sn_r"], h1)

            pe.wait_ge(dec["prep_v"], 4)
            with pe.Fori(0, HEADS - 1) as h:
                head(h, True)
            head(HEADS - 1, False)

            def dense(src, in_sem, in_value, used, slot_of, half, between=None):
                for kk in range(8):
                    c = half * 8 + kk
                    s = slot_of(c)
                    pe.wait_ge(in_sem[s], in_value(c))
                    if kk == 7 and src is mixT:
                        pe.wait_ge(E["mixB_r"], HEADS)
                    wv = slot(s).rearrange("p (k n) -> p k n", k=2)
                    for kp in range(2):
                        k = 2 * kk + kp
                        for t in range(2):
                            for n in range(2):
                                mm(ps[:, 2 * t + n, :], src[:, k, t * P:(t + 1) * P], wv[:, kp, n * 512:(n + 1) * 512],
                                   k == 0, k == KT - 1)
                    for kp in range(2):
                        for n in range(2):
                            g = 2 * kp + n
                            last = mm(ps[32 * g:32 * g + 32, 4, :], src[:, 2 * kk + kp, PROMPT:TOK],
                                      wv[:, kp, n * 512:(n + 1) * 512], kk == 0, kk == 7)
                    last.then_inc(used, 1)
                    if between:
                        between(kk)

            def routed(k):
                if k == 0:
                    pe.wait_ge(G["smp_add"], 1)
                if k < KT:
                    tile_transposes(1, x, [k], D_BANKS)
                if k == 1:
                    pe.wait_ge(ld["ld_route"], 16 * 5)
                if k:
                    pe.wait_ge(norm["tile_out_v" if k % 2 else "tile_out_a"], 8 + (k - 1) // 2 + 1)
                    return mm(ps[0:GROUPS + EXPERTS, 7, 0:TOK], wr[:, k - 1, :], hT[:, k - 1, :], k == 1, k == KT)

            for half in range(2):
                if half:
                    pe.wait_ge(G["out_add"], 1)
                    pe.wait_ge(G["smp_cp"], 1)
                dense(mixT, ring_in, lambda c: 16 * (HEADS + 1 + c // SLOTS) if c % SLOTS < PIECES else 16 * (1 + c // SLOTS),
                      G["out_used"], lambda c: c % SLOTS, half,
                      (lambda kk: routed(kk)) if half else None)

            pe.wait_ge(G["out_add"], 2)
            pe.wait_ge(G["smp_add"], 2)
            for k in range(KT // 2, KT + 1):
                last = routed(k)
            last.then_inc(R["lgT_mm"], 1)
            pe.wait_ge(R["lgT_r"], 1)
            for t, (off, n) in enumerate(TILES):
                last = tr(ps[0:n, 0, t * 36:(t + 1) * 36], lgT[:, off:off + n], GROUPS + EXPERTS)
            last.then_inc(R["route_mm"], 1)
            pe.wait_ge(R["asg_r"], 1)
            a0, a1, a2 = asg[:, 0, :], asg[:, 1, :], asg[0:SAMPLE, 2, :]
            mm(ps[:, 1, 0:32], C("before"), a0)
            mm(ps[:, 1, 32:64], C("ones"), a0, True, False)
            mm(ps[:, 1, 32:64], C("before"), a1, False, True)
            mm(ps[0:SAMPLE, 1, 64:96], C("ones", P, SAMPLE), a0, True, False)
            mm(ps[0:SAMPLE, 1, 64:96], C("ones", P, SAMPLE), a1, False, False)
            mm(ps[0:SAMPLE, 1, 64:96], C("before", SAMPLE, SAMPLE), a2, False, True)
            mm(ps[:, 1, 96:128], C("ones"), a0, True, False)
            mm(ps[:, 1, 96:128], C("ones"), a1, False, False)
            mm(ps[:, 1, 96:128], C("ones", SAMPLE), a2, False, True).then_inc(R["route_mm"], 1)

            pe.wait_ge(norm["hnorm"], 6)
            pe.wait_ge(R["rounds_r"], 1)
            rounds = pe.value_load(rnd_i[0:1, 0:1], min_val=1, max_val=MAX_ROUNDS)

            def gather(nn, banks):
                for n in nn:
                    for t, (off, m) in enumerate(TILES):
                        last = mm(ps[:, banks[n], :], Pm[0:m, t, :], hn[0:m, t, n * 512:(n + 1) * 512], t == 0, t == 2)
                return last

            def expert_inputs(v_a, v_v):
                pe.wait_ge(M["xgB_v"], v_v)
                pe.wait_ge(M["xgB_a"], v_a)
                for j in range(4):
                    xv = xg[:, j * 512:(j + 1) * 512].rearrange("s (q i) -> s i q", i=4)
                    for i in range(4):
                        last = tr(ps[:, 4 + j, i * P:(i + 1) * P], xv[:, i, :], P)
                last.then_inc(M["xT_T"], 1)

            BANK = (0, 1, 6, 7)
            with pe.Fori(0, rounds) as r:
                q1 = pe.snap(r * (PAIRS + 1) + 1)
                n0 = pe.snap(r * PAIRS)
                pe.wait_ge(M["add2"], pe.snap(n0 + 1))
                pe.wait_ge(M["P_r"], q1)
                gather((0, 1), BANK).then_inc(M["gathA"], 1)
                gather((2, 3), BANK).then_inc(M["gathB"], 1)
                expert_inputs(q1, q1)
                with pe.Fori(0, PAIRS) as it:
                    n0 = pe.snap(r * PAIRS + it)
                    n1 = pe.snap(n0 + 1)
                    q1 = pe.snap(r * (PAIRS + 1) + it + 1)
                    q2 = pe.snap(q1 + 1)
                    in1 = pe.snap((n0 * 2 + 1) * 16)
                    in2 = pe.snap((n0 * 2 + 2) * 16)

                    def landed(c):
                        s = (MOE_SLOT + c) % SLOTS
                        b = RING_BASE[s] * 16
                        return ring_in[s], (moe_v[b, c // SLOTS])

                    moe_v = {(b, q): pe.snap((in1, in2)[q] + b) for b in sorted({16 * v for v in RING_BASE}) for q in range(2)}
                    pe.wait_ge(M["WP_r"], q1)
                    pe.wait_ge(M["add2"], n1)
                    for t, (off, m) in enumerate(TILES):
                        last = pe.transpose(ps[:, 2, off:off + m], WP[0:m, t, :], C("ident", m, m))
                    last.then_inc(M["wpt_T"], 1)
                    pe.wait_ge(M["xT_r"], q1)
                    for ex in range(2):
                        for j in range(4):
                            for u in range(2):
                                sm, v = landed(8 * ex + 2 * j + u)
                                pe.wait_ge(sm, v)
                            for i in range(4):
                                k = 4 * j + i
                                for u in range(2):
                                    s = (MOE_SLOT + 8 * ex + 2 * j + u) % SLOTS
                                    last = mm(ps[64 * u:64 * u + 64, 4 + ex, :], xT[:, k, ex * CAP:(ex + 1) * CAP],
                                              slot(s)[:, i * 512:(i + 1) * 512], k == 0, k == KT - 1)
                                    if i == 3:
                                        last.then_inc(M["used"], 1)
                    pe.wait_ge(M["s0"], n1)
                    pe.wait_ge(M["wpt_cp"], n1)
                    for i in range(4):
                        last = tr(ps[:, 2, i * P:(i + 1) * P], gu[:, 0, :].rearrange("s (q i) -> s i q", i=4)[:, i, :], P)
                    last.then_inc(M["gT0"], 1)
                    pe.wait_ge(M["P_r"], q2)
                    gather((0, 1), BANK).then_inc(M["gathA"], 1)
                    pe.wait_ge(M["s1"], n1)
                    for i in range(4):
                        last = tr(ps[:, 3, i * P:(i + 1) * P], gu[:, 1, :].rearrange("s (q i) -> s i q", i=4)[:, i, :], P)
                    last.then_inc(M["gT1"], 1)
                    gather((2, 3), BANK).then_inc(M["gathB"], 1)
                    pe.wait_ge(M["xgA_v"], q2)
                    pe.wait_ge(M["xgA_a"], q2)
                    pe.wait_ge(M["h0"], n1)
                    pe.wait_ge(M["h1"], n1)
                    for i in range(4):
                        for ex in range(2):
                            sm, v = landed(16 + 2 * i + ex)
                            pe.wait_ge(sm, v)
                        for n in range(4):
                            for ex in range(2):
                                s = (MOE_SLOT + 16 + 2 * i + ex) % SLOTS
                                last = mm(ps[64 * ex:64 * ex + 64, n, :], hx[:, ex, i, :], slot(s)[:, n * 512:(n + 1) * 512],
                                          i == 0, i == 3)
                                if n == 3:
                                    last.then_inc(M["used"], 1)
                    expert_inputs(q2, q2)
                    pe.wait_ge(M["y_v"], n1)
                    pe.wait_ge(M["y_a"], n1)
                    for t, (off, m) in enumerate(TILES):
                        if t == 1:
                            pe.wait_ge(M["xT_r"], q2)
                        if t == 2:
                            pe.wait_ge(M["add0"], n1)
                        for n in range(4):
                            last = mm(ps[0:m, (t % 2) * 4 + n, :], wpT[:, off:off + m], yx[:, n * 512:(n + 1) * 512])
                        last.then_inc(M[f"c{t}"], 1)

            pe.wait_ge(M["moe_v"], 1)
            tile_transposes(2, x, range(KT), range(8))
            transposed(2)
            pe.wait_ge(F["p_in"], 32)
            for t, (off, n) in enumerate(TILES):
                for k in range(2):
                    last = tr(ps[:, 5 + k, off:off + n], pin[0:n, t, k * P:(k + 1) * P], n)
            last.then_inc(F["pT_T"], 1)

            def embedding(half, kk):
                if kk not in (2, 4):
                    return
                n = kk // 2 - 1
                if half == 0 and n == 0:
                    pe.wait_ge(F["wp_in"], 16)
                    pe.wait_ge(F["pT_r"], 1)
                c0 = half * 1024 + n * 512
                for t, (off, m) in enumerate(TILES):
                    q = half * 6 + n * 3 + t
                    if q >= 3:
                        pe.wait_ge(F["pp_r"], q - 2)
                    for k in range(2):
                        last = mm(ps[0:m, 5 + t, :], pT[:, k, off:off + m], wp[:, k, c0:c0 + 512], k == 0, k == 1)
                    last.then_inc(F["pp_mm"], 1)

            for half in range(2):
                if half:
                    embedding(1, 2)
                    pe.wait_ge(F["sg_r"], 2)
                    pe.wait_ge(F["sigs_r"], 1)
                dense(hT, ring_in, lambda c: pe.snap(rounds * (2 * PAIRS * 16) + 16 * (RING_BASE[tail_slot(c)] + 1 + c // TAIL_SLOTS)),
                      F["gate_used"], tail_slot, half, lambda kk: None if half and kk == 2 else embedding(half, kk))

        @block.scalar
        def _(act):
            def f(out, in_, func=ACT.Copy, **kw):
                return act.activation(out, in_, func, **kw)

            for dst, src in ((cwr[:, :], d["conv_w"].rearrange("l w (t p) -> (l w t) p", p=P)),
                             (grow[0:KT, :], d["g_mix"].rearrange("l (k p) -> (l k) p", p=P)),
                             (grow[KT:2 * KT, :], d["g_ffn"].rearrange("l (k p) -> (l k) p", p=P)),
                             (grow[2 * KT:3 * KT, :], d["g_ple"].rearrange("l (k p) -> (l k) p", p=P))):
                act.dma_start(dst, src).then_inc(ld["ld_conv"], 16)
            ac = Chain(act, act_chain)

            def rstd(pairs, n, signal, func=None):
                for out, in_, rows in pairs:
                    last = f(out, in_, ACT.Ln, scale=1.0 / n, bias=eps[0:rows, :])
                ac(last)
                ac.wait()
                for out, _, _ in pairs:
                    last = f(out, out, ACT.Exp, scale=-0.5)
                last.then_inc(signal, 1)

            def rms(junk=lambda t: hn[:, t, :], ready=lambda t: None):
                for t, (_, n) in enumerate(TILES):
                    ready(t)
                    last = f(junk(t)[0:n, :], x[0:n, t, :], ACT.Square, accum_out=ss[0:n, t:t + 1])
                ac(last)
                ac.wait()
                rstd([(rs2[:, :], ss[:, :], P)], D_MODEL, norm["rstd"])

            def tiles_out(ph, k0=0, k1=KT, banks=range(8)):
                for k in range(k0 + 1, k1, 2):
                    act.wait_ge(norm["tile_T"], KT * ph + k + 1)
                    f(hT[:, k, :], ps[:, banks[k % len(banks)], 0:TOK], scale=gT[:, ph, k:k + 1]).then_inc(norm["tile_out_a"], 1)

            act.wait_ge(norm["ss_zero"], 1)
            rms(ready=lambda t: act.wait_ge(ld[f"ld_x{t}"], 16))
            act.dma_start(wab[:, :, :], w_in[:, :, 6 * WIDTH:6 * WIDTH + 2 * HEADS]).then_inc(ld["ld_small"], 16)
            act.dma_start(alog[:, :], d["a_log"].to_broadcast([P, HEADS])).then_inc(ld["ld_small"], 16)
            act.dma_start(dtb[:, :], d["dt_bias"].to_broadcast([P, HEADS])).then_inc(ld["ld_small"], 16)
            act.dma_start(goutT[:, :], d["g_out"].rearrange("l (p a) -> p (l a)", a=1)).then_inc(ld["ld_small"], 16)
            act.dma_start(gJ[:, :].rearrange("p (j i) -> p j i", i=4),
                          d["g_ffn"].rearrange("l (j p i) -> p (l j) i", p=P, i=4)).then_inc(ld["ld_route"], 16)
            act.dma_start(wr[:, :, 0:GROUPS], d["w_group"].rearrange("l (k p) e -> p (l k) e", p=P)).then_inc(ld["ld_route"], 16)
            act.dma_start(wr[:, :, GROUPS:], d["w_router"].rearrange("l (k p) e -> p (l k) e", p=P)).then_inc(ld["ld_route"], 16)
            act.dma_start(rbias[:, 0:GROUPS], d["b_group"].to_broadcast([P, GROUPS])).then_inc(ld["ld_route"], 16)
            act.dma_start(rbias[:, GROUPS:], d["b_router"].to_broadcast([P, EXPERTS])).then_inc(ld["ld_route"], 16)
            act.wait_ge(dec["prep_v"], 1)
            tiles_out(0)
            def piece_out(s, this, before):
                bank = ps[:, s % 2, :]
                act.wait_ge(piece_mm, this)
                if s <= V:
                    if before is not None:
                        act.wait_ge(E["cs_r"], before)
                        act.wait_ge(E["conv_r"], before)
                    f(raw[:, s, PAD:S_AT], bank[:, 0:PROMPT])
                    last = f(raw[:, s, S_AT:RAW].rearrange("p (b c) -> p b c", c=SROW)[:, :, PAD:],
                             bank[:, PROMPT:TOK].rearrange("p (b c) -> p b c", c=SEQ_LEN))
                elif s == VA:
                    if before is not None:
                        act.wait_ge(E["vaT_T"], before)
                    last = f(vaT, bank[:, 0:TOK], ACT.Gelu_apprx_tanh)
                elif s == U:
                    last = f(uT, bank[:, 0:TOK], ACT.Gelu_apprx_tanh)
                else:
                    last = f(zs, bank[:, 0:TOK], ACT.Silu)
                last.then_inc(piece_ev, 1)

            for s in range(2):
                piece_out(s, s + 1, None)
            act.wait_ge(ld["ld_small"], 16 * 4)
            act.wait_ge(dec["prep_v"], 2)
            f(ngexp[:, :], alog[:, :], ACT.Exp)
            f(pre[:, 4], ab[:, :, HEADS:], ACT.Exp, scale=-1.0)
            f(pre[:, 3], pre[:, 2], ACT.Exp, scale=-1.0).then_inc(dec["prep_a"], 1)
            act.wait_ge(dec["prep_a"], 1)
            f(pre[:, 7], pre[:, 3], ACT.Ln, bias=1.0).then_inc(dec["prep_a"], 1)
            for s in range(2, AHEAD):
                piece_out(s, s + 1, None)
            act.wait_ge(dec["prep_v"], 4)
            f(pre[:, 1], pre[:, 5], ACT.Exp)
            f(pre[:, 2], pre[:, 7], ACT.Exp).then_inc(dec["prep_a"], 1)

            def head(h, fill):
                snap = (lambda v: v) if isinstance(h, int) else act.snap
                if not isinstance(h, int):
                    ac.base, ac.n = act.snap(h * A_CHAIN + n_before), 0
                start = ac.n
                h1 = snap(h + 1)
                step = [0]

                def pieces_out():
                    for i, at in enumerate(piece_at(FILL if fill else LAST_FILL)):
                        if at == step[0]:
                            piece_out((AHEAD + i) % PIECES, snap(h * PIECES + (AHEAD + i + 1)), h1)
                    step[0] += 1

                act.wait_ge(E["cs_T"], h1)
                f(csT[0:27, :, :], ps[0:27, 4, 0:3 * P].rearrange("r (s n) -> r s n", s=3)).then_inc(E["cs_cp"], 1)
                pieces_out()
                act.wait_ge(E["conv_r"], h1)
                f(qkvT[:, :, 0:PROMPT], acc[:, :, 0:PROMPT], ACT.Silu)
                for s in range(3):
                    last = f(qkvT[:, s, PROMPT:TOK].rearrange("p (b c) -> p b c", c=SEQ_LEN),
                             acc_s[:, s], ACT.Silu)
                last.then_inc(E["qkv_r"], 1)
                act.wait_ge(E["qkv_r"], h1)
                f(sq[:, :, :], qkvT[:, 0:2, :], ACT.Square).then_inc(E["sq_r"], 1)
                act.wait_ge(E["ln_d"], h1)
                for t, (_, n) in enumerate(TILES):
                    last = f(lnj[0:n, t, :], vd[0:n, t, :], ACT.Square, accum_out=lnr[0:n, t:t + 1])
                ac(last)
                act.wait_ge(E["ss_mm"], h1)
                rstd([(rn[:, 0, :], ps[:, 2, 0:TOK], P), (rn[:, 1, :], ps[:, 4, 0:TOK], P)], 1, E["rn_r"])
                ac.wait()
                rstd([(lnq[:, :], lnr[:, :], P)], P, E["ln_sq"])
                pieces_out()
                act.wait_ge(E["dd_r"], h1)
                f(eG, ps[:, 2, 0:TOK], ACT.Exp)
                f(Dm[:, :, :], dd[:, :, :], ACT.Exp, scale=-1.0)
                f(Ds[0:SAMPLE, :], dds[0:SAMPLE, :], ACT.Exp, scale=-1.0).then_inc(E["D_r"], 1)
                for t, (_, n) in enumerate(TILES):
                    kt, vt = ps[0:n, 5, t * P:(t + 1) * P], ps[0:n, 6, t * P:(t + 1) * P]
                    f(kbg[0:n, t, :], kt, scale=hs[0:n, t, 3:4])
                    f(kd[0:n, t, :], kt, scale=hs[0:n, t, 4:5])
                    last = f(vb[0:n, t, :], vt, scale=hs[0:n, t, 2:3])
                last.then_inc(E["tok_cp"], 1)
                pieces_out()
                act.wait_ge(E["AT_mm"], h1)
                f(QKT[:, :, :], ps[:, 6, 0:256].rearrange("p (t n) -> p t n", t=2))
                f(QKTs[0:SAMPLE, :], ps[0:SAMPLE, 6, 256:256 + SAMPLE]).then_inc(E["QKT_r"], 1)
                pieces_out()
                for lev in range(1, LEVELS):
                    v = snap(h * (LEVELS - 1) + lev)
                    act.wait_ge(lev_mm, v)
                    last = f(T1[:, :, :], ps[:, 5, 0:256].rearrange("p (t n) -> p t n", t=2))
                    if lev == 1:
                        last = f(T1s[0:SAMPLE, :], ps[0:SAMPLE, 5, 256:256 + SAMPLE])
                    last.then_inc(lev_cp, 1)
                    pieces_out()
                    if lev == 2:
                        act.wait_ge(E["W_T"], h1)
                        f(WT, ps[:, 2, 0:P]).then_inc(E["WT_r"], 1)
                    pieces_out()
                act.wait_ge(E["uw_mm"], h1)
                f(us[:, :, :], ps[:, 5, 0:256].rearrange("p (t n) -> p t n", t=2))
                f(uTs, ps[:, 5, PROMPT:TOK])
                f(WQ[:, :, 0:SEQ_LEN], ps[:, 6, PROMPT:TOK].rearrange("p (b c) -> p b c", c=SEQ_LEN))
                f(wT[:, 1, :], ps[:, 6, P:2 * P]).then_inc(E["uw_cp"], 1)
                pieces_out()
                act.wait_ge(E["S1_mm"], h1)
                f(S1, ps[:, 7, 0:P]).then_inc(E["S1_r"], 1)
                pieces_out()
                act.wait_ge(E["vnTT"], h1)
                f(vns[0:SAMPLE, :], ps[0:SAMPLE, 5, 0:P]).then_inc(E["vns_r"], 1)
                pieces_out()
                act.wait_ge(E["o_mm"], h1)
                f(oS, ps[:, 4, 0:TOK]).then_inc(E["os_p"], 1)
                pieces_out()
                act.wait_ge(E["os_r"], h1)
                f(osq, oS, ACT.Square).then_inc(E["osq_r"], 1)
                act.wait_ge(E["oss_mm"], h1)
                rstd([(orn, ps[:, 3, 0:TOK], P)], P, E["or_r"])
                pieces_out()
                pieces_out()
                act.wait_ge(E["cs_st"], snap(h * 96 + 96))
                act.wait_ge(E["mixA_r"], h1)
                act.wait_ge(E["mixB_r"], h1)
                assert ac.n - start == A_CHAIN, ac.n - start

            act.wait_ge(dec["prep_v"], 5)
            n_before = ac.n
            with act.Fori(0, HEADS - 1) as h:
                head(h, True)
            ac.base, ac.n = None, n_before + (HEADS - 1) * A_CHAIN
            head(HEADS - 1, False)

            def sample_copies(sem_):
                for g in range(4):
                    last = f(smp[0:SAMPLE, g, :], ps[32 * g:32 * g + 32, 4, :])
                last.then_inc(sem_, 1)

            def half_squares(t, c0, sums):
                n = TILES[t][1]
                return f(hn[0:n, t, c0:c0 + 1024], x[0:n, t, c0:c0 + 1024], ACT.Square, accum_out=sums[0:n, t:t + 1])

            act.wait_ge(E["mixB_r"], HEADS)
            act.wait_ge(E["cs_st"], 6 * 16 * HEADS)
            act.wait_ge(E["va_st"], 16 * HEADS)
            act.wait_ge(E["s2_st"], 16 * HEADS + 1)
            act.wait_ge(E["sn_st"], 16 * HEADS + 1)
            act.dma_start(pin[:, 0:2, :], d["p_prompt"].rearrange("l b (t p) n -> p (l b t) n", p=P)).then_inc(F["p_in"], 16)
            act.dma_start(pin[0:SAMPLE, 2, :], d["p_sample"].rearrange("l b t n -> (l b t) n")).then_inc(F["p_in"], 16)
            for half in range(2):
                act.wait_ge(G["out_used"], 8 * (half + 1))
                if half:
                    act.wait_ge(G["smp_add"], 1)
                sample_copies(G["smp_cp"])
                if not half:
                    act.wait_ge(G["out_add"], 1)
                    act.wait_ge(G["smp_add"], 1)
                    for t in range(3):
                        last = half_squares(t, 0, ss_a)
                    ac(last)
                    ac.wait()
                    ac(f(ln_b[:, :], ss_a[:, :], scale=1.0 / D_MODEL, bias=EPS))
                    tiles_out(1, 0, KT // 2, D_BANKS)

            act.wait_ge(G["out_add"], 2)
            act.wait_ge(G["smp_add"], 2)
            act.wait_ge(G["smp_cp"], 2)
            for q in range(4):
                tiles_out(1, KT // 2 + 2 * q, KT // 2 + 2 * q + 2, D_BANKS)
                if q < 3:
                    last = half_squares(q, 1024, ss)
            ac(last)
            act.wait_ge(R["lgT_mm"], 1)
            f(lgT, ps[0:GROUPS + EXPERTS, 7, 0:TOK]).then_inc(R["lgT_r"], 1)
            ac.wait()
            for t in range(3):
                last = f(rs2[:, t:t + 1], ss[:, t:t + 1], ACT.Ln, scale=1.0 / D_MODEL, bias=ln_b[:, t:t + 1])
            ac(last)
            ac.wait()
            f(rs2[:, :], rs2[:, :], ACT.Exp, scale=-0.5).then_inc(norm["rstd"], 1)
            act.wait_ge(norm["rstd"], 2)
            for t, (_, n) in enumerate(TILES):
                f(hn[0:n, t, :], x[0:n, t, :], scale=rs2[0:n, t:t + 1]).then_inc(norm["hnorm"], 1)
            act.wait_ge(R["route_in"], 1)
            f(rt[:, 1, :, 0:4], rt[:, 0, :, 0:4], ACT.Exp).then_inc(R["route_exp"], 1)
            act.wait_ge(R["route_in"], 2)
            f(rc[:, 5, :], rc[:, 4, :], ACT.Exp).then_inc(R["route_exp"], 1)

            act.wait_ge(R["rounds_r"], 1)
            rounds = act.value_load(rnd_i[0:1, 0:1], min_val=1, max_val=MAX_ROUNDS)

            def rows_out(j, bank):
                return f(xg[:, j * 512:(j + 1) * 512], ps[:, bank, :])

            with act.Fori(0, rounds) as r:
                q1 = act.snap(r * (PAIRS + 1) + 1)
                act.wait_ge(M["gathA"], q1)
                rows_out(1, 1).then_inc(M["xgA_a"], 1)
                act.wait_ge(M["gathB"], q1)
                rows_out(3, 7).then_inc(M["xgB_a"], 1)
                with act.Fori(0, PAIRS) as it:
                    n1 = act.snap(r * PAIRS + it + 1)
                    q2 = act.snap(r * (PAIRS + 1) + it + 2)
                    u0 = act.snap((r * PAIRS + it) * 24 + 8)
                    u1 = act.snap(u0 + 8)
                    u2 = act.snap(u0 + 16)
                    act.wait_ge(M["wpt_T"], n1)
                    f(wpT[:, :], ps[:, 2, 0:TOK]).then_inc(M["wpt_cp"], 1)
                    act.wait_ge(M["used"], u0)
                    f(gu[:, 0, :], ps[:, 4, :]).then_inc(M["s0"], 1)
                    act.wait_ge(M["gT0"], n1)
                    f(sg[:, 0], ps[:, 2, :].rearrange("p (i s) -> p i s", i=4)[:, :, 0:CAP], ACT.Silu).then_inc(M["silu0"], 1)
                    act.wait_ge(M["used"], u1)
                    f(gu[:, 1, :], ps[:, 5, :]).then_inc(M["s1"], 1)
                    act.wait_ge(M["gathA"], q2)
                    rows_out(1, 1).then_inc(M["xgA_a"], 1)
                    act.wait_ge(M["gT1"], n1)
                    f(sg[:, 1], ps[:, 3, :].rearrange("p (i s) -> p i s", i=4)[:, :, 0:CAP], ACT.Silu).then_inc(M["silu1"], 1)
                    act.wait_ge(M["gathB"], q2)
                    rows_out(3, 7).then_inc(M["xgB_a"], 1)
                    act.wait_ge(M["used"], u2)
                    f(yx[:, 512:1024], ps[:, 1, :])
                    f(yx[:, 1536:2048], ps[:, 3, :]).then_inc(M["y_a"], 1)
                    act.wait_ge(M["h1"], n1)

            act.wait_ge(M["moe_v"], 1)
            tiles_out(2)
            act.wait_ge(F["pT_T"], 1)
            for k in range(2):
                last = f(pT[:, k, :], ps[:, 5 + k, 0:TOK])
            last.then_inc(F["pT_r"], 1)
            rms()
            act.wait_ge(norm["rstd"], 3)

            def gates(t):
                f(sig[:, 2 * t:2 * t + 2, :], ps[:, 2 * t:2 * t + 2, :], ACT.Sigmoid, scale=rs2[:, t:t + 1]).then_inc(F["sg_r"], 1)

            for half in range(2):
                act.wait_ge(F["gate_used"], 8 * (half + 1))
                if half:
                    act.wait_ge(F["x_new"], 3)
                gates(0)
                sample_copies(F["sigs_r"])
                gates(1)
                act.wait_ge(F["ssum"], half + 1)
                f(smp[0:SAMPLE, 0:2, :], smp[0:SAMPLE, 0:2, :], ACT.Sigmoid, scale=rs2[0:SAMPLE, 2:3]).then_inc(F["ssg_r"], 1)
            rms(lambda t: squares[t], lambda t: act.wait_ge(F["x_new"], 3 + t + 1))
            act.wait_ge(norm["rstd"], 4)
            act.wait_ge(F["xg_r"], 2)
            f(y[1], y[1], scale=rs2[:, 1:2]).then_inc(F["y1_r"], 1)

        @block.vector
        def _(v):
            ch = Chain(v, vec_chain)
            ts, tt, st, cp = v.tensor_scalar, v.tensor_tensor, v.scalar_tensor_tensor, v.tensor_copy

            def seq(*makers):
                for m in makers:
                    ch(m())
                    ch.wait()

            def normalised_rows():
                for t, (_, n) in enumerate(TILES):
                    ts(hn[0:n, t, :], x[0:n, t, :], rs2[0:n, t:t + 1], None, ALU.mult).then_inc(norm["hnorm"], 1)

            def tiles_out(ph, k0=0, k1=KT, banks=range(8)):
                for k in range(k0, k1, 2):
                    v.wait_ge(norm["tile_T"], KT * ph + k + 1)
                    ts(hT[:, k, :], ps[:, banks[k % len(banks)], 0:TOK], gT[:, ph, k:k + 1], None, ALU.mult).then_inc(norm["tile_out_v"], 1)

            v.memset(eps[:, :], EPS)
            v.memset(lnr[:, :], 1.0)
            v.memset(ss_a[:, :], 1.0)
            v.memset(ss[:, :], 1.0).then_inc(norm["ss_zero"], 1)
            v.memset(lnm[:, :], 0.0)
            v.memset(ab[:, :, :], 0.0)
            v.memset(zero[:, :], 0.0).then_inc(E["s2_st"], 1)
            v.memset(lns[:, :], 0.0).then_inc(E["sn_st"], 1)
            v.memset(lnq[:, :], 0.0).then_inc(M["add2"], 1)
            v.memset(pre[:, :, :, :], 0.0)
            ch(v.memset(raw[:, :, 0:PAD], 0.0))
            v.wait_ge(dec["prep_mm"], 1)
            cp(cw[:, :, :, :], ps[:, 7, 0:96].rearrange("p (w s h) -> p w s h", w=TAPS, s=3))
            cp(gT[:, :, :], ps[:, 7, 96:144].rearrange("p (a k) -> p a k", a=3)).then_inc(dec["prep_v"], 1)
            v.wait_ge(dec["prep_v"], 1)
            for t in range(3):
                v.wait_ge(ld[f"ld_x{t}"], 16)
            v.wait_ge(norm["rstd"], 1)
            normalised_rows()
            tiles_out(0)
            v.wait_ge(ld["ld_small"], 16 * 4)
            v.wait_ge(dec["prep_mm"], 2)
            cp(ab[:, 0:2, :], ps[:, 2, 0:32].rearrange("p (t c) -> p t c", t=2))
            ch(cp(ab[0:SAMPLE, 2, :], ps[0:SAMPLE, 2, 32:48]))
            ch.wait()
            for t in range(3):
                last = tt(pre[:, 1, t, :], ab[:, t, 0:HEADS], dtb[:, :], ALU.add)
            ch(last)
            ch.wait()
            st(out=pre[:, 2], in0=pre[:, 1], scalar=-1.0, in1=pre[:, 1], op0=ALU.mult, op1=ALU.max).then_inc(dec["prep_v"], 1)
            v.wait_ge(dec["prep_a"], 2)
            ch(ts(pre[:, 4], pre[:, 4], 1.0, None, ALU.add))
            ch(st(out=pre[:, 6], in0=pre[:, 1], scalar=0.0, in1=pre[:, 7], op0=ALU.max, op1=ALU.add))
            ch.wait()
            ch(v.reciprocal(pre[:, 3], pre[:, 4]))
            for t in range(3):
                last = st(out=pre[:, 0, t, :], in0=pre[:, 6, t, :], scalar=-1.0, in1=ngexp[:, :], op0=ALU.mult, op1=ALU.mult)
            last.then_inc(dec["prep_v"], 1)
            v.wait_ge(dec["prep_v"], 3)
            v.wait_ge(dec["prep_mm"], 3)
            cp(pre[:, 5, 0:2, :], ps[:, 3, 0:16].rearrange("p (t c) -> p t c", t=2))
            cp(pre[0:SAMPLE, 5, 2, :], ps[0:SAMPLE, 3, 16:24])
            cp(pre[:, 6, 0:2, :], ps[:, 3, 24:40].rearrange("p (t c) -> p t c", t=2))
            ch(cp(pre[0:SAMPLE, 6, 2, :], ps[0:SAMPLE, 3, 40:48]))
            ch.wait()
            tt(pre[:, 7, 0:2], pre[:, 6, 0:2], pre[:, 5, 0:2], ALU.subtract)
            v.memset(pre[:, 7, 2], 0.0)
            ch(v.memset(zero[:, :], 0.0))
            ch.wait()
            tt(pre[0:SAMPLE, 7, 2], pre[0:SAMPLE, 6, 2], pre[0:SAMPLE, 5, 2], ALU.subtract).then_inc(dec["prep_v"], 1)
            v.wait_ge(dec["prep_a"], 3)
            ch(tt(pre[:, 4], pre[:, 3], pre[:, 1], ALU.mult))
            ch.wait()
            for kind, src in enumerate((0, 5, 3, 4, 2)):
                last = cp(sc[:, :, :, kind].rearrange("p h t -> p t h"), pre[:, src])
            last.then_inc(dec["prep_v"], 1)
            v.wait_ge(dec["prep_v"], 5)
            n_before = ch.n

            def head(h, loop):
                snap = v.snap if loop else (lambda a: a)
                if loop:
                    ch.base, ch.n = v.snap(h * V_CHAIN + n_before), 0
                start = ch.n
                h1 = snap(h + 1)
                cp(hs[:, :, :], sc[:, bass.ds(h, 1), :, :].rearrange("p a t k -> p (a t) k"))
                ch(cp(hcw[:, :, :], cw[:, :, :, bass.ds(h, 1)].rearrange("p w s a -> p w (s a)")))
                ch.wait()
                for t, (_, n) in enumerate(TILES):
                    ts(gcol[0:n, t, :], C("ones", n), hs[0:n, t, 0:1], None, ALU.mult)
                v.wait_ge(E["st_T"], h1)
                cp(raw_s[:, :, :, 0:PAD],
                   ps[:, 2, 0:72].rearrange("p (s b c) -> p s b c", s=3, c=PAD)).then_inc(E["st_in"], 1)
                v.wait_ge(piece_ev, snap(h * PIECES + (V + 1)))
                v.wait_ge(E["st_in"], h1)
                cp(cs[:, :, 0:PAD], raw[:, :, PROMPT:PROMPT + PAD])
                cp(cs[:, :, PAD:].rearrange("p s (b c) -> p s b c", c=PAD), raw_s[:, :, :, SEQ_LEN:]).then_inc(E["cs_r"], 1)
                for s in range(3):
                    ch(ts(acc[:, s, 0:RAW - PAD], raw[:, s, 0:RAW - PAD], hcw[:, 0, s:s + 1], None, ALU.mult))
                for j in range(1, TAPS):
                    ch.wait()
                    for s in range(3):
                        last = st(out=acc[:, s, 0:RAW - PAD], in0=raw[:, s, j:j + RAW - PAD], scalar=hcw[:, j, s:s + 1],
                                  in1=acc[:, s, 0:RAW - PAD], op0=ALU.mult, op1=ALU.add)
                        if s == 2 and j == TAPS - 1:
                            last.then_inc(E["conv_r"], 1)
                        else:
                            ch(last)
                v.wait_ge(E["vaT_T"], h1)
                v.tensor_reduce(lnm[:, 0:2], ps[:, 3, 0:256].rearrange("p (t n) -> p t n", t=2), AX, ALU.add)
                ch(v.tensor_reduce(lnm[0:SAMPLE, 2:3], ps[0:SAMPLE, 3, 256:384], AX, ALU.add))
                ch.wait()
                ch(ts(lns[:, :], lnm[:, :], -1.0 / P, None, ALU.mult))
                ch.wait()
                for t, (_, n) in enumerate(TILES):
                    last = ts(vd[0:n, t, :], ps[0:n, 3, t * P:(t + 1) * P], lns[0:n, t:t + 1], None, ALU.add)
                last.then_inc(E["ln_d"], 1)
                v.wait_ge(E["rn_r"], h1)
                st(out=qk[:, 0, :], in0=qkvT[:, 0, :], scalar=float(P) ** -0.5, in1=rn[:, 0, :], op0=ALU.mult, op1=ALU.mult)
                tt(qk[:, 1, :], qkvT[:, 1, :], rn[:, 1, :], ALU.mult).then_inc(E["qk_r"], 1)
                v.wait_ge(E["tok_mm"], h1)
                for t in range(2):
                    ts(dd[:, t, :], ps[:, 2, t * P:(t + 1) * P], hs[:, t, 1:2], 0.0, ALU.subtract, ALU.max)
                ts(dds[0:SAMPLE, :], ps[0:SAMPLE, 2, PROMPT:TOK], hs[0:SAMPLE, 2, 1:2], 0.0, ALU.subtract,
                   ALU.max).then_inc(E["dd_r"], 1)
                v.wait_ge(E["qk_r"], h1)
                v.wait_ge(E["D_r"], h1)
                tt(qg, qk[:, 0, :], eG, ALU.mult)
                for t in range(2):
                    tt(DS[:, t, :], Dm[:, t, :], C("strict"), ALU.mult)
                    tt(DC[:, t, :], Dm[:, t, :], C("causal"), ALU.mult)
                tt(DSs[0:SAMPLE, :], Ds[0:SAMPLE, :], C("bstrict", SAMPLE), ALU.mult)
                ch(tt(DCs[0:SAMPLE, :], Ds[0:SAMPLE, :], C("bcausal", SAMPLE), ALU.mult))
                ch.wait()
                for t in range(2):
                    st(out=Am[:, t, :], in0=ps[:, 7, t * P:(t + 1) * P], scalar=hs[:, t, 2:3], in1=DS[:, t, :],
                       op0=ALU.mult, op1=ALU.mult)
                tt(QKm[:, :, :], ps[:, 7, 256:512].rearrange("p (t n) -> p t n", t=2), DC[:, :, :], ALU.mult)
                st(out=Ams[0:SAMPLE, :], in0=ps[0:SAMPLE, 4, 0:SAMPLE], scalar=hs[0:SAMPLE, 2, 2:3], in1=DSs[0:SAMPLE, :],
                   op0=ALU.mult, op1=ALU.mult)
                tt(QKms[0:SAMPLE, :], ps[0:SAMPLE, 4, SAMPLE:2 * SAMPLE], DCs[0:SAMPLE, :], ALU.mult).then_inc(E["A_r"], 1)
                v.wait_ge(E["A_r"], h1)
                for t in range(2):
                    st(out=X[:, t, :], in0=Am[:, t, :], scalar=-1.0, in1=C("low0"), op0=ALU.mult, op1=ALU.mult)
                ch(st(out=Xs[0:SAMPLE, :], in0=Ams[0:SAMPLE, :], scalar=-1.0, in1=C("low0", SAMPLE, SAMPLE), op0=ALU.mult,
                      op1=ALU.mult))
                v.wait_ge(E["AT_mm"], h1)
                for lev in range(LEVELS):
                    for t in range(2):
                        last = tt(NT[:, lev, t, :], ps[:, 5, t * P:(t + 1) * P], C(f"mt{lev}"), ALU.mult)
                for lev in range(2):
                    last = tt(NTs[0:SAMPLE, lev, :], ps[0:SAMPLE, 5, 256:256 + SAMPLE], C(f"mt{lev}", SAMPLE, SAMPLE), ALU.mult)
                ch(last)
                ch.wait()
                for t in range(2):
                    tt(X[:, t, :], X[:, t, :], C("ident"), ALU.add)
                    st(out=XT[:, t, :], in0=NT[:, 0, t, :], scalar=-1.0, in1=C("ident"), op0=ALU.mult, op1=ALU.add)
                tt(Xs[0:SAMPLE, :], Xs[0:SAMPLE, :], C("ident", SAMPLE, SAMPLE), ALU.add)
                st(out=XTs[0:SAMPLE, :], in0=NTs[0:SAMPLE, 0, :], scalar=-1.0, in1=C("ident", SAMPLE, SAMPLE), op0=ALU.mult,
                   op1=ALU.add).then_inc(E["NT_r"], 1)
                v.wait_ge(E["NT_r"], h1)
                for lev in range(1, LEVELS):
                    if lev > 1:
                        v.wait_ge(lev_new, snap(h * (LEVELS - 1) + lev - 1))
                    lv = snap(h * (LEVELS - 1) + lev)
                    v.wait_ge(lev_x, lv)
                    two = lambda b: ps[:, b, 0:256].rearrange("p (t n) -> p t n", t=2)
                    if lev < LEVELS - 1:
                        tt(X[:, :, :], X[:, :, :], two(6), ALU.subtract)
                    if lev == 1:
                        tt(XTs[0:SAMPLE, :], XTs[0:SAMPLE, :], ps[0:SAMPLE, 7, 256:256 + SAMPLE], ALU.subtract)
                    tt(XT[:, :, :], XT[:, :, :], two(7), ALU.subtract).then_inc(lev_new, 1)
                    if lev == 1:
                        w48 = snap(h * 48 + 48)
                        v.wait_ge(E["w_ld"], w48)
                        tt(Wm, Wh, C("causal"), ALU.mult).then_inc(E["W_r"], 1)
                        v.wait_ge(E["ln_sq"], h1)
                        for t, (_, n) in enumerate(TILES):
                            last = st(out=vn[0:n, t, :], in0=vd[0:n, t, :], scalar=lnq[0:n, t:t + 1], in1=gB[0:n, :],
                                      op0=ALU.mult, op1=ALU.mult)
                        last.then_inc(E["vn_r"], 1)
                    if lev == 3:
                        v.wait_ge(E["Wrep"], h1)
                        for b in range(SEQS):
                            last = tt(WTs[0:SAMPLE, b * 4:b * 4 + 4], ps[0:SAMPLE, 3, 0:SEQ_LEN],
                                      C("ball", SAMPLE)[:, b * 4:b * 4 + 4], ALU.mult)
                        last.then_inc(E["WTs_r"], 1)
                    if lev == 5:
                        v.wait_ge(E["mixA_mm"], h1)
                        for t in range(2):
                            tt(mA[:, t * P:(t + 1) * P], ps[:, 4, t * P:(t + 1) * P], bB, ALU.add)
                        for b in range(SEQS):
                            at = PROMPT + b * SEQ_LEN
                            last = tt(mA[:, at:at + SEQ_LEN], ps[:, 4, at:at + SEQ_LEN], bB[:, 0:SEQ_LEN], ALU.add)
                        ch(last)
                        ch.wait()
                        v.wait_ge(piece_ev, snap(h * PIECES + (U + 1)))
                        tt(mixT[:, bass.ds(h, 1), :].rearrange("p a n -> p (a n)"), mA, uT, ALU.mult).then_inc(E["mixA_r"], 1)
                cp(WQ[:, :, SEQ_LEN:], qg[:, PROMPT:TOK].rearrange("p (b c) -> p b c", c=SEQ_LEN)).then_inc(E["WQ_r"], 1)
                v.wait_ge(E["SQ_mm"], h1)
                SQ = ps[:, 2, 0:64].rearrange("p (b c) -> p b c", c=8)
                sq4 = lambda a: a.rearrange("p (b c) -> p b c", c=SEQ_LEN)
                tt(sq4(vnTs), sq4(uTs), SQ[:, :, 0:SEQ_LEN], ALU.subtract).then_inc(E["vnT_r"], 1)
                v.wait_ge(E["wS_mm"], h1)
                tt(vn1, us[:, 1, :], ps[:, 3, 0:P], ALU.subtract).then_inc(E["vn1_r"], 1)
                v.wait_ge(E["vns_r"], h1)
                for b in range(SEQS):
                    last = ts(Vm[0:SAMPLE, b, :], vns[0:SAMPLE, :], C("seq", SAMPLE)[:, b:b + 1], None, ALU.mult)
                last.then_inc(E["Vm_r"], 1)
                v.wait_ge(E["os_p"], h1)
                os4 = sq4(oS[:, PROMPT:TOK])
                tt(os4, os4, SQ[:, :, SEQ_LEN:], ALU.add).then_inc(E["os_r"], 1)
                v.wait_ge(E["s2_st"], snap(h * 16 + 1))
                st(out=S2, in0=S1, scalar=eG[:, 2 * P - 1:2 * P], in1=ps[:, 7, P:2 * P], op0=ALU.mult,
                   op1=ALU.add).then_inc(E["S2_r"], 1)
                v.wait_ge(E["dS_mm"], h1)
                v.wait_ge(E["sn_st"], snap(h * 16 + 1))
                for b in range(SEQS):
                    at = PROMPT + b * SEQ_LEN + SEQ_LEN - 1
                    last = st(out=Snew[:, b, :], in0=Sold[:, b, :], scalar=eG[:, at:at + 1],
                              in1=ps[:, 5 + b // 4, (b % 4) * P:(b % 4 + 1) * P], op0=ALU.mult, op1=ALU.add)
                last.then_inc(E["Sn_r"], 1)
                v.wait_ge(piece_ev, snap((h + 1) * PIECES))
                v.wait_ge(E["osq_r"], h1)
                ch(st(out=ot, in0=oS, scalar=goutT[:, 0:1], in1=zs, op0=ALU.mult, op1=ALU.mult))
                ch.wait()
                v.wait_ge(E["or_r"], h1)
                tt(mixT[:, bass.ds(h + HEADS, 1), :].rearrange("p a n -> p (a n)"), ot, orn, ALU.mult).then_inc(E["mixB_r"], 1)
                v.wait_ge(E["mixB_r"], h1)
                v.wait_ge(E["va_st"], snap(h * 16 + 16))
                assert ch.n - start == V_CHAIN, ch.n - start

            with v.Fori(0, HEADS - 1) as h:
                head(h, True)
            ch.base, ch.n = None, n_before + (HEADS - 1) * V_CHAIN
            head(HEADS - 1, False)

            for half in range(2):
                c0 = half * 1024
                v.wait_ge(G["out_used"], 8 * (half + 1))
                for t in range(2):
                    for n in range(2):
                        xs = x[:, t, c0 + n * 512:c0 + (n + 1) * 512]
                        last = tt(xs, xs, ps[:, 2 * t + n, :], ALU.add)
                last.then_inc(G["out_add"], 1)
                v.wait_ge(G["smp_cp"], half + 1)
                xs = x[0:SAMPLE, 2, c0:c0 + 1024].rearrange("p (n c) -> p n c", n=2)
                ch(tt(xs, xs, smp[0:SAMPLE, 0:2, :], ALU.add))
                ch.wait()
                tt(xs, xs, smp[0:SAMPLE, 2:4, :], ALU.add).then_inc(G["smp_add"], 1)
                if not half:
                    tiles_out(1, 0, KT // 2, D_BANKS)

            v.wait_ge(G["out_add"], 2)
            v.wait_ge(G["smp_add"], 2)
            tiles_out(1, KT // 2, KT, D_BANKS)
            v.memset(lg[:, :, :], 0.0)
            v.memset(rankm[:, :, :], FAR)
            ch(v.memset(wt[:, :, :], 0.0))
            ch.wait()
            v.wait_ge(ld["ld_route"], 16 * 5)
            v.wait_ge(norm["rstd"], 2)
            v.wait_ge(R["route_mm"], 1)
            for t, (_, n) in enumerate(TILES):
                last = st(out=lg[0:n, t, :], in0=ps[0:n, 0, t * 36:(t + 1) * 36], scalar=rs2[0:n, t:t + 1], in1=rbias[0:n, :],
                          op0=ALU.mult, op1=ALU.add)
            ch(last)
            ch.wait()
            gl, el = lg[:, :, 0:GROUPS], lg[:, :, GROUPS:]
            c3 = lambda a, n: a.unsqueeze(2).to_broadcast([P, 3, n])

            def first_max(val, n, mx, one):
                t = rt[:, 2, :, 0:n]
                seq(lambda: v.tensor_reduce(mx, val, AX, ALU.max),
                    lambda: tt(t, val, c3(mx, n), ALU.is_equal))
                for q in range(3):
                    last = st(out=rt[:, 3, q, 0:n], in0=rt[:, 2, q, 0:n], scalar=-99.0, in1=C("iota99")[:, 0:n],
                              op0=ALU.mult, op1=ALU.add)
                ch(last)
                ch.wait()
                seq(lambda: v.tensor_reduce(rc[:, 1, :], rt[:, 3, :, 0:n], AX, ALU.min),
                    lambda: tt(one, rt[:, 3, :, 0:n], c3(rc[:, 1, :], n), ALU.is_equal))

            first_max(gl, GROUPS, rc[:, 0, :], rt[:, 4, :, 0:GROUPS])
            tt(rt[:, 0, :, 0:4], gl, c3(rc[:, 0, :], GROUPS), ALU.subtract).then_inc(R["route_in"], 1)
            ch(ts(rt[:, 4, :, 8:12], rt[:, 4, :, 0:GROUPS], 1e30, -1e30, ALU.mult, ALU.add))
            ch.wait()
            for g in range(GROUPS):
                sl = slice(g * PER_GROUP, (g + 1) * PER_GROUP)
                last = tt(rt[:, 5, :, sl], el[:, :, sl], rt[:, 4, :, g:g + 1].to_broadcast([P, 3, PER_GROUP]), ALU.mult)
            ch(last)
            ch.wait()
            for g in range(GROUPS):
                sl = slice(g * PER_GROUP, (g + 1) * PER_GROUP)
                last = tt(rt[:, 6, :, sl], rt[:, 5, :, sl], rt[:, 4, :, 8 + g:9 + g].to_broadcast([P, 3, PER_GROUP]), ALU.add)
            ch(last)
            ch.wait()
            first_max(rt[:, 6], EXPERTS, rc[:, 3, :], rt[:, 7])
            seq(lambda: st(out=rt[:, 5], in0=rt[:, 7], scalar=-3e30, in1=rt[:, 6], op0=ALU.mult, op1=ALU.add))
            first_max(rt[:, 5], EXPERTS, rc[:, 6, :], rt[:, 8])
            tt(rc[:, 4, :], rc[:, 6, :], rc[:, 3, :], ALU.subtract).then_inc(R["route_in"], 1)
            tt(asg[:, :, :], rt[:, 7], rt[:, 8], ALU.add).then_inc(R["asg_r"], 1)
            v.wait_ge(R["route_exp"], 1)
            seq(lambda: v.tensor_reduce(rc[:, 7, :], rt[:, 1, :, 0:4], AX, ALU.add),
                lambda: v.reciprocal(rc[:, 2, :], rc[:, 7, :]))
            v.wait_ge(R["route_exp"], 2)
            seq(lambda: ts(rc[:, 8, :], rc[:, 5, :], 1.0, None, ALU.add),
                lambda: v.reciprocal(rc[:, 9, :], rc[:, 8, :]),
                lambda: tt(rc[:, 10, :], rc[:, 9, :], rc[:, 2, :], ALU.mult),
                lambda: tt(rc[:, 11, :], rc[:, 10, :], rc[:, 5, :], ALU.mult))
            tt(rt[:, 7], rt[:, 7], c3(rc[:, 10, :], EXPERTS), ALU.mult)
            seq(lambda: tt(rt[:, 8], rt[:, 8], c3(rc[:, 11, :], EXPERTS), ALU.mult),
                lambda: tt(wt[:, :, 0:EXPERTS], rt[:, 7], rt[:, 8], ALU.add))
            v.wait_ge(R["asg_r"], 1)
            v.wait_ge(R["route_mm"], 2)
            ch(v.tensor_reduce(cnt[:, :], ps[:, 1, 96:128], AX, ALU.max))
            ch(ts(rt[:, 3], asg[:, :, :], -FAR, FAR, ALU.mult, ALU.add))
            ch.wait()
            for t, (_, n) in enumerate(TILES):
                last = tt(rankm[0:n, t, 0:EXPERTS], rt[0:n, 3, t, :], ps[0:n, 1, t * 32:(t + 1) * 32], ALU.add)
            ch(last)
            for q in range(1, MAX_ROUNDS):
                last = ts(rnd[:, q:q + 1], cnt[:, :], float(CAP * q), None, ALU.is_gt)
            ch(last)
            ch(v.memset(rnd[:, 0:1], 1.0))
            ch.wait()
            seq(lambda: v.tensor_reduce(cnt[:, :], rnd[:, :], AX, ALU.add))
            cp(rnd_i[:, :], cnt[:, :]).then_inc(R["rounds_r"], 1)
            v.wait_ge(R["rounds_r"], 1)

            rounds = v.value_load(rnd_i[0:1, 0:1], min_val=1, max_val=MAX_ROUNDS)

            def one_hots(e0):
                for t, (_, n) in enumerate(TILES):
                    for ex in range(2):
                        last = ts(Pm[0:n, t, ex * CAP:(ex + 1) * CAP], C("iota", n), rankm[0:n, t, bass.ds(e0 + ex, 1)],
                                  None, ALU.is_equal)
                last.then_inc(M["P_r"], 1)

            def weighted(e0):
                for t, (_, n) in enumerate(TILES):
                    for ex in range(2):
                        last = ts(WP[0:n, t, ex * CAP:(ex + 1) * CAP], C("iota", n), rankm[0:n, t, bass.ds(e0 + ex, 1)],
                                  wt[0:n, t, bass.ds(e0 + ex, 1)], ALU.is_equal, ALU.mult)
                last.then_inc(M["WP_r"], 1)

            def rows_out(j, bank):
                return cp(xg[:, j * 512:(j + 1) * 512], ps[:, bank, :])

            def xT_out():
                for j in range(4):
                    for i in range(4):
                        k = 4 * j + i
                        last = ts(xT[:, k, :], ps[:, 4 + j, i * P:(i + 1) * P], gJ[:, k:k + 1], None, ALU.mult)
                last.then_inc(M["xT_r"], 1)

            with v.Fori(0, rounds) as r:
                q1 = v.snap(r * (PAIRS + 1) + 1)
                n0 = v.snap(r * PAIRS)
                one_hots(0)
                weighted(0)
                v.wait_ge(M["gathA"], q1)
                rows_out(0, 0).then_inc(M["xgA_v"], 1)
                v.wait_ge(M["gathB"], q1)
                rows_out(2, 6).then_inc(M["xgB_v"], 1)
                v.wait_ge(M["xT_T"], q1)
                xT_out()
                with v.Fori(0, PAIRS) as it:
                    n1 = v.snap(r * PAIRS + it + 1)
                    q2 = v.snap(r * (PAIRS + 1) + it + 2)
                    u2 = v.snap((r * PAIRS + it) * 24 + 24)
                    e2 = v.snap(it * 2 + 2)
                    one_hots(e2)
                    v.wait_ge(M["wpt_T"], n1)
                    weighted(e2)
                    v.wait_ge(M["silu0"], n1)
                    tt(hx[:, 0], sg[:, 0], ps[:, 2, :].rearrange("p (i s) -> p i s", i=4)[:, :, CAP:], ALU.mult).then_inc(M["h0"], 1)
                    v.wait_ge(M["gathA"], q2)
                    rows_out(0, 0).then_inc(M["xgA_v"], 1)
                    v.wait_ge(M["silu1"], n1)
                    tt(hx[:, 1], sg[:, 1], ps[:, 3, :].rearrange("p (i s) -> p i s", i=4)[:, :, CAP:], ALU.mult).then_inc(M["h1"], 1)
                    v.wait_ge(M["gathB"], q2)
                    rows_out(2, 6).then_inc(M["xgB_v"], 1)
                    v.wait_ge(M["used"], u2)
                    cp(yx[:, 0:512], ps[:, 0, :])
                    cp(yx[:, 1024:1536], ps[:, 2, :]).then_inc(M["y_v"], 1)
                    v.wait_ge(M["xT_T"], q2)
                    xT_out()
                    v.wait_ge(M["add2"], n1)
                    for t, (_, n) in enumerate(TILES):
                        v.wait_ge(M[f"c{t}"], n1)
                        for c in range(2):
                            xs = x[0:n, t, c * 1024:(c + 1) * 1024].rearrange("p (a b) -> p a b", a=2)
                            b0 = (t % 2) * 4 + 2 * c
                            last = tt(xs, xs, ps[0:n, b0:b0 + 2, :], ALU.add)
                        last.then_inc(M[f"add{t}"], 1)
                e_end = v.snap((r + 1) * (PAIRS + 1))
                v.wait_ge(M["P_r"], e_end)
                v.wait_ge(M["WP_r"], e_end)
                ts(rankm[:, :, :], rankm[:, :, :], -float(CAP), None, ALU.add).then_inc(M["rank_r"], 1)
                v.wait_ge(M["rank_r"], v.snap(r + 1))
                v.wait_ge(M["add2"], v.snap((r + 1) * PAIRS + 1))
            v.memset(zero[:, :], 0.0).then_inc(M["moe_v"], 1)

            tiles_out(2)
            v.wait_ge(norm["rstd"], 3)
            for half in range(2):
                c0 = half * 1024
                for n in range(2):
                    for t, (_, m) in enumerate(TILES):
                        v.wait_ge(F["pp_mm"], half * 6 + n * 3 + t + 1)
                        cp(tmp[0:m, t, n * 512:(n + 1) * 512], ps[0:m, 5 + t, :]).then_inc(F["pp_r"], 1)
                v.wait_ge(F["pp_r"], 6 * (half + 1))
                for t, (_, m) in enumerate(TILES):
                    if t == 1:
                        v.wait_ge(F["sigs_r"], half + 1)
                        tt(smp[0:SAMPLE, 0:2, :], smp[0:SAMPLE, 0:2, :], smp[0:SAMPLE, 2:4, :], ALU.add).then_inc(F["ssum"], 1)
                    if t < 2:
                        v.wait_ge(F["sg_r"], 2 * half + t + 1)
                        gate = sig[:, 2 * t:2 * t + 2, :]
                    else:
                        v.wait_ge(F["ssg_r"], half + 1)
                        gate = smp[0:SAMPLE, 0:2, :]
                    part = tmp[0:m, t, :].rearrange("p (n c) -> p n c", n=2)
                    ch(tt(part, part, gate, ALU.mult))
                    ch.wait()
                    xs = x[0:m, t, c0:c0 + 1024]
                    tt(xs, xs, tmp[0:m, t, :], ALU.add).then_inc(F["x_new"], 1)
                v.wait_ge(F["x_new"], 3 * (half + 1))
            v.wait_ge(F["gf_in"], 16)
            for t, (_, n) in enumerate(TILES):
                tt(y[t][0:n, :], x[0:n, t, :], gfin[0:n, :], ALU.mult).then_inc(F["xg_r"], 1)
            v.wait_ge(F["xg_r"], 3)
            v.wait_ge(norm["rstd"], 4)
            for t in (0, 2):
                n = TILES[t][1]
                ts(y[t][0:n, :], y[t][0:n, :], rs2[0:n, t:t + 1], None, ALU.mult).then_inc(F["y_r"], 1)


_INS = ["x_prompt", "x_sample", "state_conv", "state_delta", "p_prompt", "p_sample", "w_in", "w_s", "b_s", "g_v", "g_mix",
        "conv_w", "a_log", "dt_bias", "g_out", "w_out", "g_ffn", "w_group", "b_group", "w_router", "b_router", "w_gate",
        "w_up", "w_down", "g_ple", "w_ple_gate", "w_ple", "g_final"]
_OUTS = [(1, PROMPT, D_MODEL), (SEQS, SEQ_LEN, D_MODEL), (1, 1, PAD, CONV_DIM), (1, 1, HEADS, P, P),
         (1, SEQS, PAD, CONV_DIM), (1, SEQS, HEADS, P, P), (1, SEQS, SEQ_LEN, WIDTH)]


def kernel(**inputs):
    import concourse.bacc as _bacc
    from concourse.bass_utils import run_bass_kernel_spmd as _run

    nc = _bacc.Bacc("TRN2", target_bir_lowering=False, num_devices=1)
    arrays, d = {}, {}
    for name in _INS:
        a = np.ascontiguousarray(inputs[name])
        arrays[f"in_{name}_dram"] = a
        d[name] = nc.dram_tensor(f"in_{name}_dram", a.shape, F32, kind="ExternalInput").ap()
    arrays["in_consts_dram"] = _constants()
    d["consts"] = nc.dram_tensor("in_consts_dram", (P, N_CONST), F32, kind="ExternalInput").ap()
    outs = [nc.dram_tensor(f"out_{i}_dram", shape, F32, kind="ExternalOutput").ap() for i, shape in enumerate(_OUTS)]
    trunk(nc, d, outs)
    r = _run(nc, [arrays], core_ids=[0])
    return tuple(r.results[0][f"out_{i}_dram"] for i in range(len(_OUTS)))
```
